# Optimizing a Trainium2 kernel written in Bass

```python
import math
import jax, jax.numpy as jnp
from jax import lax
import numpy as np

D_MODEL = 1024
BATCH = 1
SEQ = 2048
DEPTH = 1

HEAD_DIM = 64
N_HEADS_A = 8
N_KV_A = 2
N_HEADS_B = 8
D_A = N_HEADS_A * HEAD_DIM
D_KV_A = N_KV_A * HEAD_DIM
D_B = N_HEADS_B * HEAD_DIM
D_MIX = D_A + D_B
D_IN = D_A + 2 * D_KV_A + 3 * D_B
D_FF = 4 * D_MODEL
D_PLE = 256
GRID_W = 64
ROPE_THETA = 10000.0
ROPE_HALF = HEAD_DIM // 2
Q_BLOCK = 128
DILATED_PATTERNS = ((128, 1), (512, 4), (2048, 16))
N_BUCKETS = 32
MAX_DISTANCE = 1024
EPS = 1e-6
NEG_BIG = -1e30

kernel_name = "hymba_axial_gqa_dilated_swa_encoder_layer"

def rms_norm(x, g):
    xf = x.astype(jnp.float32)
    y = xf * lax.rsqrt(jnp.mean(xf * xf, axis=-1, keepdims=True) + EPS)
    return (y * g.astype(jnp.float32)).astype(x.dtype)

def axial_rope_tables(n_tokens):
    rows = n_tokens // GRID_W
    row = jnp.broadcast_to(jnp.arange(rows)[:, None], (rows, GRID_W)).reshape(-1).astype(jnp.float32)
    col = jnp.broadcast_to(jnp.arange(GRID_W)[None, :], (rows, GRID_W)).reshape(-1).astype(jnp.float32)
    n_axis = ROPE_HALF // 2
    inv_freq = ROPE_THETA ** (-jnp.arange(n_axis, dtype=jnp.float32) / n_axis)
    ang = jnp.concatenate([row[:, None] * inv_freq, col[:, None] * inv_freq], axis=-1)
    return jnp.cos(ang), jnp.sin(ang)

def apply_rope(x, cos, sin):
    xf = x.astype(jnp.float32)
    x1, x2 = xf[..., :ROPE_HALF], xf[..., ROPE_HALF:]
    c, s = cos[None, :, None, :], sin[None, :, None, :]
    return jnp.concatenate([x1 * c - x2 * s, x2 * c + x1 * s], axis=-1).astype(x.dtype)

def mixer_a(q, k, v, g_q, g_k, cos, sin):
    q = apply_rope(rms_norm(q, g_q), cos, sin)
    k = apply_rope(rms_norm(k, g_k), cos, sin)
    b, s_len = q.shape[0], q.shape[1]
    grp = N_HEADS_A // N_KV_A
    nblk = s_len // Q_BLOCK
    qb = q.reshape(b, nblk, Q_BLOCK, N_KV_A, grp, HEAD_DIM).transpose(1, 0, 2, 3, 4, 5)
    scale = HEAD_DIM ** -0.5

    def block(q_blk):
        sc = jnp.einsum('bqkgd,bskd->bkgqs', q_blk, k, preferred_element_type=jnp.float32) * scale
        pr = jax.nn.softmax(sc, axis=-1)
        return jnp.einsum('bkgqs,bskd->bqkgd', pr.astype(v.dtype), v)

    o = lax.map(block, qb)
    return o.transpose(1, 0, 2, 3, 4, 5).reshape(b, s_len, D_A)

def t5_bucket(rel):
    nb = N_BUCKETS // 2
    max_exact = nb // 2
    side = jnp.where(rel > 0, nb, 0)
    n = jnp.abs(rel)
    large = max_exact + (jnp.log(jnp.maximum(n, max_exact).astype(jnp.float32) / max_exact)
                         / math.log(MAX_DISTANCE / max_exact) * (nb - max_exact)).astype(jnp.int32)
    large = jnp.minimum(large, nb - 1)
    return side + jnp.where(n < max_exact, n, large)

def dilated_pattern(q, k, v, rel_bias, window, dilation):
    b, s_len, h, d = q.shape
    length = s_len // dilation
    half = window // (2 * dilation)
    blk = half
    nblk = -(-length // blk)
    lp = nblk * blk

    def to_sub(x):
        x = x.reshape(b, length, dilation, h, d).transpose(0, 2, 1, 3, 4)
        return jnp.pad(x, ((0, 0), (0, 0), (0, lp - length), (0, 0), (0, 0)))

    def band(x):
        xp = jnp.pad(to_sub(x), ((0, 0), (0, 0), (blk, blk), (0, 0), (0, 0)))
        xb = xp.reshape(b, dilation, nblk + 2, blk, h, d)
        return jnp.concatenate([xb[:, :, :-2], xb[:, :, 1:-1], xb[:, :, 2:]], axis=3)

    qs = to_sub(q).reshape(b, dilation, nblk, blk, h, d)
    ks, vs = band(k), band(v)
    qi = jnp.arange(blk)
    kj = jnp.arange(3 * blk)
    rel = kj[None, :] - blk - qi[:, None]
    key_m = jnp.arange(nblk)[:, None] * blk - blk + kj[None, :]
    valid = ((jnp.abs(rel) <= half)[None, :, :]
             & (key_m >= 0)[:, None, :] & (key_m < length)[:, None, :])
    bias = rel_bias[t5_bucket(rel * dilation)].astype(jnp.float32)
    bias = bias.transpose(0, 2, 1)[None, None, None]
    sc = jnp.einsum('brnqhd,brnkhd->brnqhk', qs, ks, preferred_element_type=jnp.float32) * (HEAD_DIM ** -0.5)
    sc = jnp.where(valid[None, None, :, :, None, :], sc + bias, NEG_BIG)
    mx = jnp.max(sc, axis=-1)
    e = jnp.exp(sc - mx[..., None])
    den = jnp.sum(e, axis=-1)
    o = jnp.einsum('brnqhk,brnkhd->brnqhd', e.astype(vs.dtype), vs,
                   preferred_element_type=jnp.float32) / den[..., None]

    def from_sub(y):
        y = y.reshape((b, dilation, lp) + y.shape[4:])[:, :, :length]
        return jnp.moveaxis(y, 1, 2).reshape((b, s_len) + y.shape[3:])

    return from_sub(o), from_sub(mx), from_sub(den)

def mixer_b(q, k, v, rel_bias):
    outs, mxs, dens = [], [], []
    for window, dilation in DILATED_PATTERNS:
        o, mx, den = dilated_pattern(q, k, v, rel_bias, window, dilation)
        outs.append(o); mxs.append(mx); dens.append(den)
    m_all = jnp.maximum(jnp.maximum(mxs[0], mxs[1]), mxs[2])
    w = [den * jnp.exp(mx - m_all) for den, mx in zip(dens, mxs)]
    w_sum = w[0] + w[1] + w[2]
    y = (w[0][..., None] * outs[0] + w[1][..., None] * outs[1] + w[2][..., None] * outs[2]) / w_sum[..., None]
    b, s_len = q.shape[0], q.shape[1]
    return y.reshape(b, s_len, D_B).astype(q.dtype)

def setup_inputs(seed: int = 0) -> dict:
    key = jax.random.key(seed)
    ks = jax.random.split(key, 20)
    nrm = lambda k, shape, scale: jax.random.normal(k, shape, jnp.float32) * scale
    gain = lambda k, shape: 1.0 + 0.05 * jax.random.normal(k, shape, jnp.float32)
    return {
        "x": nrm(ks[0], (BATCH, SEQ, D_MODEL), 1.0),
        "p": nrm(ks[1], (DEPTH, BATCH, SEQ, D_PLE), 1.0),
        "w_in": nrm(ks[2], (DEPTH, D_MODEL, D_IN), D_MODEL ** -0.5),
        "g_attn_pre": gain(ks[3], (DEPTH, D_MODEL)),
        "g_q": gain(ks[4], (DEPTH, HEAD_DIM)),
        "g_k": gain(ks[5], (DEPTH, HEAD_DIM)),
        "g_out_a": gain(ks[6], (DEPTH, D_A)),
        "g_out_b": gain(ks[7], (DEPTH, D_B)),
        "w_out": nrm(ks[8], (DEPTH, D_MIX, D_MODEL), D_MIX ** -0.5),
        "g_attn_post": gain(ks[9], (DEPTH, D_MODEL)),
        "rel_bias": nrm(ks[10], (N_BUCKETS, N_HEADS_B), 0.5),
        "g_mlp_pre": gain(ks[11], (DEPTH, D_MODEL)),
        "w_ff1": nrm(ks[12], (DEPTH, D_MODEL, D_FF), D_MODEL ** -0.5),
        "w_ff2": nrm(ks[13], (DEPTH, D_FF, D_MODEL), D_FF ** -0.5),
        "g_mlp_post": gain(ks[14], (DEPTH, D_MODEL)),
        "g_ple": gain(ks[15], (DEPTH, D_MODEL)),
        "w_ple_gate": nrm(ks[16], (DEPTH, D_MODEL, D_MODEL), D_MODEL ** -0.5),
        "w_ple_proj": nrm(ks[17], (DEPTH, D_PLE, D_MODEL), D_PLE ** -0.5),
    }

def reference(x, p, w_in, g_attn_pre, g_q, g_k, g_out_a, g_out_b, w_out, g_attn_post, rel_bias,
              g_mlp_pre, w_ff1, w_ff2, g_mlp_post, g_ple, w_ple_gate, w_ple_proj):
    b, s_len = x.shape[0], x.shape[1]
    cos, sin = axial_rope_tables(s_len)
    split_at = [D_A, D_A + D_KV_A, D_A + 2 * D_KV_A, D_A + 2 * D_KV_A + D_B, D_A + 2 * D_KV_A + 2 * D_B]
    h = x
    for i in range(DEPTH):
        xn = rms_norm(h, g_attn_pre[i])
        proj = jnp.einsum('bsd,de->bse', xn, w_in[i])
        qa, ka, va, qb, kb, vb = jnp.split(proj, split_at, axis=-1)
        ya = mixer_a(qa.reshape(b, s_len, N_HEADS_A, HEAD_DIM),
                     ka.reshape(b, s_len, N_KV_A, HEAD_DIM),
                     va.reshape(b, s_len, N_KV_A, HEAD_DIM), g_q[i], g_k[i], cos, sin)
        yb = mixer_b(qb.reshape(b, s_len, N_HEADS_B, HEAD_DIM),
                     kb.reshape(b, s_len, N_HEADS_B, HEAD_DIM),
                     vb.reshape(b, s_len, N_HEADS_B, HEAD_DIM), rel_bias)
        y = jnp.concatenate([rms_norm(ya, g_out_a[i]), rms_norm(yb, g_out_b[i])], axis=-1)
        y = jnp.einsum('bse,ed->bsd', y, w_out[i])
        h = h + rms_norm(y, g_attn_post[i])
        xn = rms_norm(h, g_mlp_pre[i])
        f = jnp.square(jax.nn.relu(jnp.einsum('bsd,df->bsf', xn, w_ff1[i])))
        f = jnp.einsum('bsf,fd->bsd', f, w_ff2[i])
        h = h + rms_norm(f, g_mlp_post[i])
        gate = jax.nn.sigmoid(jnp.einsum('bsd,de->bse', rms_norm(h, g_ple[i]), w_ple_gate[i]))
        h = h + gate * jnp.einsum('bsp,pd->bsd', p[i], w_ple_proj[i])
    return h


_drawn_inputs = setup_inputs


def setup_inputs(seed=0):
    import zlib

    import numpy as np

    out = dict(_drawn_inputs(seed))
    spreads = {}
    factors = {'g_ple': 23.875}
    for name, (base, spread) in spreads.items():
        noise = np.random.default_rng([zlib.crc32(name.encode()), seed]).standard_normal(out[name].shape)
        drawn = base * np.exp(spread * noise) if base else spread * noise
        out[name] = __import__('jax').numpy.asarray(drawn.astype(out[name].dtype))
    for name, factor in factors.items():
        out[name] = (out[name] * factor).astype(out[name].dtype)
    return out
```

```python
import math
from contextlib import ExitStack

import numpy as np

import concourse.bass as bass
from concourse import mybir
from concourse.alu_op_type import AluOpType as ALU

F32 = mybir.dt.float32
F32R = mybir.dt.float32r
ACT = mybir.ActivationFunctionType
AXX = mybir.AxisListType.X

P = 128
D = 1024
S = 2048
HD = 64
NHA, NKV, NHB = 8, 2, 8
D_AB = 512
D_IN = 2304
D_FF = 4096
D_PLE = 256
KD = D // P
BT = 512
TT = BT // P
NBLK = S // BT
RES = 4
SUB = S // RES
PAD = 16
EPS = 1e-6
NEG = -1e30
BANK = 512
CH = 2048
NBIAS = 33
NRAW, NSPL = 3, 2
VL = 2 * BANK
OWN_W = 7 * P
TABLE_W = OWN_W + 7 * (P + 2 * PAD)
ROWS_W = TABLE_W + 8 * P
PAIRS = ((0, 0), (0, 1), (1, 0))


class Kit:

    def __init__(self, nc, ctx, phase):
        self.nc, self.ctx, self.phase = nc, ctx, phase

    def sb(self, name, shape, dt=F32):
        return self.ctx.enter_context(self.nc.sbuf_tensor(f"{self.phase}_{name}", shape, dt))

    def banks(self, n=8):
        return [self.ctx.enter_context(self.nc.psum_tensor(f"{self.phase}_bank{i}", [P, BANK], F32)) for i in range(n)]

    def sem(self, name):
        return self.ctx.enter_context(self.nc.semaphore(f"{self.phase}_{name}"))

    def sems(self, name, n):
        return [self.sem(f"{name}{i}") for i in range(n)]


def row_broadcast(row):
    n = row.shape[-1]
    return bass.AP(row.tensor, row.offset, [[0, P], [1, n]])


def project_phase(nc, x, w_in, g_pre, g_q, g_k, rope, ident_d, rel_bias, onehot, scr):
    STEPS_1, STEPS = 4, 10
    NCH = 9
    NG = 5
    GROUP_OF = [0, 0, 1, 2, 2, 3, 3, 4, 4]
    NORM_AT = {0: (0, 1), 3: (2,), 5: (3,)}
    with ExitStack() as ctx:
        k = Kit(nc, ctx, "proj")
        ident = k.sb("ident", [P, P])
        g_row = k.sb("g_row", [P, D])
        gq_row = k.sb("gq_row", [P, HD])
        gk_row = k.sb("gk_row", [P, HD])
        rb = k.sb("rb", [NBIAS, NHB])
        oh = k.sb("oh", [NBIAS, 2, BANK])
        vec = k.sb("vec", [NHB, 2, BANK])
        x_t = k.sb("x_t", [P, TT, D])
        junk = k.sb("junk", [P, 2, D], mybir.dt.bfloat16)
        ssq = k.sb("ssq", [P, 2])
        ms = k.sb("ms", [P, 2])
        rec = k.sb("rec", [P, 2])
        rstd = k.sb("rstd", [P, 2])
        xn = k.sb("xn", [P, 2, D])
        xT = [[k.sb(f"xT{u}{h}", [P, KD, BT], F32R) for h in range(2)] for u in range(2)]
        w_raw = k.sb("w_raw", [P, NRAW, CH])
        w_sp = [k.sb(f"w_split{h}", [P, NSPL, CH], F32R) for h in range(2)]
        rope_t = k.sb("rope_t", [P, 2, TT, 2 * HD])
        qs = k.sb("qs", [P, TT, D_AB])
        ks = k.sb("ks", [P, TT, NKV * HD])
        st = k.sb("st", [P, TT, BANK])
        t1 = k.sb("t1", [P, D_AB])
        t2 = k.sb("t2", [P, D_AB])
        hs = k.sb("hs", [P, TT, 4, 8])
        qo = k.sb("qo", [P, 2, NHA * 2 * HD])
        ko = k.sb("ko", [P, 2, NKV * 2 * HD])
        zrow = k.sb("zrow", [PAD, D_AB])
        bank = k.banks()
        acc, tp, bias_bank = bank[0:4], bank[4:6], bank[6:8]

        const_in = k.sem("const_in")
        oh_dma, bias_mm, vec_done = k.sems("oh_dma", 2), k.sem("bias_mm"), k.sem("vec_done")
        bias_out = k.sems("bias_out", 2)
        sp_step, act_step, pe_step = k.sem("sp_step"), k.sem("act_step"), k.sem("pe_step")
        x_in = k.sems("x_in", TT)
        rope_in = k.sem("rope_in")
        ssq_done, rec_done, rstd_done, xn_done = (k.sem(n) for n in ("ssq_done", "rec_done", "rstd_done", "xn_done"))
        tp_done, hi_done, lo_done = (k.sem(n) for n in ("tp_done", "hi_done", "lo_done"))
        w_in_dma = k.sems("w_dma", NRAW)
        w_hi, w_lo, w_used = k.sem("w_hi"), k.sem("w_lo"), k.sem("w_used")
        pool_step = k.sem("pool_step")
        acc_done, evicted = k.sem("acc_done"), k.sem("evicted")
        qs_free = k.sem("qs_free")
        ks_free = k.sem("ks_free")
        qo_ready, ko_ready = k.sem("qo_ready"), k.sem("ko_ready")
        st_out = k.sems("st_out", TT)
        qo_out, ko_out = k.sems("qo_out", 2), k.sems("ko_out", 2)
        pad_out = k.sem("pad_out")
        z_done = k.sem("z_done")
        dve = k.sem("dve")
        head_rstd, var_step = k.sem("head_rstd"), k.sem("var_step")
        block = ctx.enter_context(nc.Block())

        @block.sync
        def _(sp):
            for t in range(TT):
                sp.dma_start(x_t[:, t, :], x[t * P:(t + 1) * P, :]).then_inc(x_in[t], 16)
                if t == 0:
                    sp.dma_start(ident[:], ident_d).then_inc(const_in, 16)
                    sp.dma_start(g_row[:], row_broadcast(g_pre)).then_inc(const_in, 16)
            sp.dma_start(gq_row[:], row_broadcast(g_q)).then_inc(const_in, 16)
            sp.dma_start(gk_row[:], row_broadcast(g_k)).then_inc(const_in, 16)
            sp.dma_start(rb[:], rel_bias).then_inc(const_in, 16)
            sp.wait_ge(z_done, 1)
            for row in (0, PAD + S):
                sp.dma_start(scr["vB"][row:row + PAD, :], zrow[:]).then_inc(pad_out, 16)
            with sp.Fori(0, NBLK // 2) as it:
                for u in range(2):
                    b = it * 2 + u
                    sp.dma_start(rope_t[:, u, :, :], rope[bass.ds(b * BT, BT), :].rearrange("(t p) c -> p t c", p=P)
                                 ).then_inc(rope_in, 16)
                    for i in range(NCH):
                        c = NCH * u + i
                        sp.wait_ge(w_lo, it * (2 * NCH) + c + 1)
                        sp.dma_start(w_raw[:, c % NRAW, :], w_in[i]).then_inc(w_in_dma[c % NRAW], 16)
                        if i % 2 == 0 and i // 2 < TT:
                            t = i // 2
                            sp.wait_ge(xn_done, b * TT + t + 1)
                            sp.dma_start(x_t[:, t, :], x[bass.ds((b + 1) * BT + t * P, P), :]).then_inc(x_in[t], 16)
                        if i % 2 == 0 and i // 2 < 4:
                            j = i // 2
                            sp.wait_ge(bias_mm, b * 4 + j + 1)
                            sp.sem_inc(sp_step, 1)
                            sp.dma_start(oh[:, j % 2, :], onehot[:, bass.ds((b * 4 + j) * BANK, BANK)]
                                         ).then_inc(oh_dma[j % 2], 16)
                        if i == 5:
                            for t in range(TT):
                                sp.wait_ge(qo_ready, b * TT + t + 1)
                                sp.dma_start(scr["qA"][bass.ds(b * BT + t * P, P), :], qo[:, t % 2, :]
                                             ).then_inc(qo_out[t % 2], 16)
                        if i == 6:
                            for t in range(TT):
                                sp.wait_ge(ko_ready, b * TT + t + 1)
                                sp.dma_start(scr["kA"][bass.ds(b * BT + t * P, P), :], ko[:, t % 2, :]
                                             ).then_inc(ko_out[t % 2], 16)
            for s in (*qo_out, *ko_out):
                sp.wait_ge(s, 16 * (2 * NBLK + 1))
            for s in st_out:
                sp.wait_ge(s, 16 * (6 * NBLK + 1))
            for s in bias_out:
                sp.wait_ge(s, 16 * (2 * NBLK + 1))
            sp.wait_ge(pad_out, 32)

        @block.gpsimd
        def _(pool):
            pool.memset(zrow[:], 0.0).then_inc(z_done, 1)
            pool.sem_inc(w_lo, NRAW)
            pool.sem_inc(w_used, 1)
            pool.sem_inc(evicted, TT)
            pool.sem_inc(qs_free, TT)
            pool.sem_inc(ks_free, TT)
            pool.sem_inc(bias_mm, 2)
            pool.sem_inc(vec_done, 2)
            for s in (*bias_out, *st_out, *qo_out, *ko_out):
                pool.sem_inc(s, 16)
            with pool.Fori(0, NBLK // 2) as it:
                for c in range(2 * NCH):
                    slot, half = c % NRAW, c % NSPL
                    pool.wait_ge(w_in_dma[slot], it * (16 * 2 * NCH // NRAW) + 16 * (c // NRAW + 1))
                    prev, pu = (c - NSPL) % NCH, (c - NSPL) // NCH
                    if prev == NCH - 1 or GROUP_OF[prev + 1] != GROUP_OF[prev]:
                        pool.wait_ge(evicted, it * (2 * NG * TT) + NG * TT * pu + TT + TT * GROUP_OF[prev] + TT)
                    else:
                        pool.wait_ge(w_used, it * 8 + 4 * pu + [0, 3, 5, 7].index(prev) + 2)
                    pool.sem_inc(pool_step, 1)
                    pool.tensor_scalar(w_sp[0][:, half, :], w_raw[:, slot, :], 1.0, 0.0, ALU.mult, ALU.add
                                       ).then_inc(w_hi, 1)
                    pool.wait_ge(w_hi, it * (2 * NCH) + c + 1)
                    pool.tensor_tensor(w_sp[1][:, half, :], w_raw[:, slot, :], w_sp[0][:, half, :].bitcast(F32),
                                       ALU.subtract).then_inc(w_lo, 1)

        @block.tensor
        def _(pe):
            def turn(nb, t):
                pe.wait_ge(xn_done, nb * TT + t + 1)
                for half in range(2):
                    if not (isinstance(nb, int) and t == 0):
                        pe.wait_ge(lo_done, (nb * TT + t) * 2 + half - 1)
                    for j in range(4):
                        kk = 4 * half + j
                        mm = pe.transpose(tp[half][:, j * P:(j + 1) * P], xn[:, t % 2, kk * P:(kk + 1) * P], ident[:])
                    mm.then_inc(tp_done, 1)

            pe.wait_ge(const_in, 80)
            for t in range(TT):
                turn(0, t)
            with pe.Fori(0, NBLK // 2) as it:
                for u in range(2):
                    b = it * 2 + u
                    pe.wait_ge(lo_done, b * (2 * TT) + 2 * TT)
                    for i in range(NCH):
                        c = NCH * u + i
                        g = GROUP_OF[i]
                        n_k = 8 if g == 1 else 4
                        width = CH // n_k
                        k0 = 4 if i > 0 and GROUP_OF[i - 1] == g else 0
                        first, last = k0 == 0, k0 + n_k == KD
                        pe.wait_ge(w_lo, it * (2 * NCH) + NRAW + c + 1)
                        w = [h[:, c % NSPL, :].rearrange("p (k n) -> p k n", k=n_k) for h in w_sp]
                        for t in range(TT):
                            if first:
                                pe.wait_ge(evicted, b * (NG * TT) + TT * g + t + 1)
                            for kk in range(n_k):
                                for q, (a, m) in enumerate(PAIRS):
                                    mm = pe.matmul(acc[t][:, 0:width], xT[u][a][:, k0 + kk, t * P:(t + 1) * P],
                                                   w[m][:, kk, :], start=first and kk == 0 and q == 0,
                                                   stop=last and kk == n_k - 1 and q == 2)
                            if last:
                                mm.then_inc(acc_done, 1)
                        if not last:
                            mm.then_inc(w_used, 1)
                        if i % 2 == 1:
                            turn(b + 1, i // 2)
                        elif i < 8:
                            part = b * 4 + i // 2
                            pe.wait_ge(oh_dma[i // 2 % 2], b * 32 + 16 * (i // 4 + 1))
                            pe.wait_ge(vec_done, part + 1)
                            pe.sem_inc(pe_step, 1)
                            pe.matmul(bias_bank[i // 2 % 2][0:NHB, :], rb[:], oh[:, i // 2 % 2, :], start=True, stop=True
                                      ).then_inc(bias_mm, 1)

        @block.scalar
        def _(act):
            def squares(nb, t):
                act.wait_ge(x_in[t], nb * 16 + 16)
                act.activation(junk[:, t % 2, :], x_t[:, t, :], ACT.Square, accum_out=ssq[:, t % 2:t % 2 + 1]).then_inc(ssq_done, 1)
                act.wait_ge(rec_done, nb * TT + t + 1)
                act.activation(rstd[:, t % 2:t % 2 + 1], rec[:, t % 2:t % 2 + 1], ACT.Sqrt).then_inc(rstd_done, 1)

            def hi_part(nb, t, par):
                for half in range(2):
                    act.wait_ge(tp_done, (nb * TT + t) * 2 + half + 1)
                    act.activation(xT[par][0][:, 4 * half:4 * half + 4, t * P:(t + 1) * P],
                                   tp[half][:].rearrange("p (k n) -> p k n", k=4), ACT.Copy).then_inc(hi_done, 1)

            squares(0, 0)
            for t in range(TT):
                if t < TT - 1:
                    squares(0, t + 1)
                hi_part(0, t, 0)
            with act.Fori(0, NBLK // 2) as it:
                for u in range(2):
                    b = it * 2 + u
                    for i in range(NCH):
                        g = GROUP_OF[i]
                        for t in NORM_AT.get(i, ()):
                            squares(b + 1, t)
                        if i == NCH - 1 or GROUP_OF[i + 1] != g:
                            for t in range(TT):
                                act.wait_ge(acc_done, b * (NG * TT) + TT * g + t + 1)
                                if g == 0:
                                    act.wait_ge(qs_free, b * TT + t + 1)
                                    act.activation(qs[:, t, :], acc[t][:], ACT.Copy).then_inc(evicted, 1)
                                elif g == 1:
                                    act.wait_ge(ks_free, b * TT + t + 1)
                                    act.wait_ge(st_out[t], b * 96 + 16)
                                    act.activation(st[:, t, 0:P], acc[t][:, P:2 * P], ACT.Copy)
                                    act.activation(ks[:, t, :], acc[t][:, 0:P], ACT.Copy).then_inc(evicted, 1)
                                    act.wait_ge(evicted, b * (NG * TT) + TT + TT * g + t + 1)
                                    act.dma_start(scr["vA"][bass.ds(b * BT + t * P, P), :], st[:, t, 0:P]
                                                  ).then_inc(st_out[t], 16)
                                else:
                                    m = g - 1
                                    act.wait_ge(st_out[t], b * 96 + 32 * m)
                                    act.activation(st[:, t, :], acc[t][:], ACT.Copy,
                                                   scale=HD ** -0.5 if g == 2 else 1.0).then_inc(evicted, 1)
                                    act.wait_ge(evicted, b * (NG * TT) + TT + TT * g + t + 1)
                                    if g == 4:
                                        act.dma_start(scr["vB"][bass.ds(b * BT + t * P + PAD, P), :], st[:, t, :]
                                                      ).then_inc(st_out[t], 16)
                                    else:
                                        rows = scr[("qB", "kB")[g - 2]][bass.ds(b * BT + t * P, P), :].rearrange(
                                            "p (h c d) -> p h c d", h=NHB, c=2)
                                        for twice in range(2):
                                            act.dma_start(rows[:, :, twice, :],
                                                          st[:, t, :].rearrange("p (h d) -> p h d", h=NHB)
                                                          ).then_inc(st_out[t], 16)
                            if g <= 1:
                                for t in range(TT):
                                    n = (NHA, NKV)[g]
                                    act.wait_ge(dve, it * (STEPS * 4 * TT) + STEPS * TT * (2 * u + g) + STEPS_1 * (t + 1))
                                    act.activation(hs[:, t, 3, 0:n], hs[:, t, 2, 0:n], ACT.Sqrt,
                                                   scale=(1.0 / HD, 1.0)[g]).then_inc(head_rstd, 1)
                        if i % 2 == 1:
                            hi_part(b + 1, i // 2, 1 - u)
                        elif i < 8:
                            part = b * 4 + i // 2
                            act.wait_ge(bias_mm, part + 3)
                            act.wait_ge(bias_out[i // 2 % 2], b * 32 + 16 * (i // 4 + 1))
                            act.activation(vec[:, i // 2 % 2, :], bias_bank[i // 2 % 2][0:NHB, :], ACT.Copy
                                           ).then_inc(vec_done, 1)
                            act.wait_ge(vec_done, part + 3)
                            act.sem_inc(act_step, 1)
                            act.dma_start(scr["bias"][:, bass.ds(part * BANK, BANK)], vec[:, i // 2 % 2, :]
                                          ).then_inc(bias_out[i // 2 % 2], 16)

        @block.vector
        def _(ve):
            def normed(nb, t):
                ve.wait_ge(ssq_done, nb * TT + t + 1)
                a, z = t % 2, t % 2 + 1
                ve.tensor_scalar(ms[:, a:z], ssq[:, a:z], 1.0 / D, EPS, ALU.mult, ALU.add).then_inc(var_step, 1)
                ve.wait_ge(var_step, nb * TT + t + 1)
                ve.reciprocal(rec[:, a:z], ms[:, a:z]).then_inc(rec_done, 1)
                ve.wait_ge(rstd_done, nb * TT + t + 1)
                if not (isinstance(nb, int) and t < 2):
                    ve.wait_ge(tp_done, (nb * TT + t) * 2 - 2)
                ve.scalar_tensor_tensor(out=xn[:, a, :], in0=x_t[:, t, :], scalar=rstd[:, a:z], in1=g_row[:],
                                        op0=ALU.mult, op1=ALU.mult).then_inc(xn_done, 1)

            def lo_part(nb, t, par):
                for half in range(2):
                    at = (slice(None), slice(4 * half, 4 * half + 4), slice(t * P, (t + 1) * P))
                    ve.wait_ge(hi_done, (nb * TT + t) * 2 + half + 1)
                    ve.tensor_tensor(xT[par][1][at], tp[half][:].rearrange("p (k n) -> p k n", k=4),
                                     xT[par][0][at].bitcast(F32), ALU.subtract).then_inc(lo_done, 1)

            def stepper(first):
                done = [0]

                def then(ins, wait=True):
                    done[0] += 1
                    ins.then_inc(dve, 1)
                    if wait:
                        ve.wait_ge(dve, first + done[0])
                return then

            def head_squares(it, u, t, q):
                n, src = (NHA, qs) if q else (NKV, ks)
                g = 0 if q else 1
                b = it * 2 + u
                then = stepper(it * (STEPS * 4 * TT) + (STEPS * TT * (2 * u + g) + STEPS_1 * t))
                x_h, y1 = src[:, t, :].rearrange("p (h d) -> p h d", h=n), t1[:, 0:n * HD].rearrange(
                    "p (h d) -> p h d", h=n)
                ve.wait_ge(evicted, b * (NG * TT) + TT + TT * g + t + 1)
                then(ve.tensor_tensor(y1, x_h, x_h, ALU.mult))
                then(ve.tensor_reduce(hs[:, t, 0, 0:n], y1, AXX, ALU.add))
                then(ve.tensor_scalar(hs[:, t, 1, 0:n], hs[:, t, 0, 0:n], 1.0 / HD, EPS, ALU.mult, ALU.add))
                then(ve.reciprocal(hs[:, t, 2, 0:n], hs[:, t, 1, 0:n]), False)

            def rotated(it, u, t, q):
                n, src, g_h, dst = (NHA, qs, gq_row, qo) if q else (NKV, ks, gk_row, ko)
                g = 0 if q else 1
                b = it * 2 + u
                then = stepper(it * (STEPS * 4 * TT) + (STEPS * TT * (2 * u + g) + STEPS_1 * TT + (STEPS - STEPS_1) * t))
                heads = lambda a: a.rearrange("p (h d) -> p h d", h=n)
                x_h, y1, y2 = heads(src[:, t, :]), heads(t1[:, 0:n * HD]), heads(t2[:, 0:n * HD])
                cos = rope_t[:, u, t:t + 1, 0:HD].broadcast_to([P, n, HD])
                sin = rope_t[:, u, t:t + 1, HD:2 * HD]
                g_all = g_h[:].unsqueeze(1).broadcast_to([P, n, HD])
                ve.wait_ge(head_rstd, b * (2 * TT) + (0 if q else TT) + t + 1)
                then(ve.tensor_tensor(y1, x_h, hs[:, t, 3, 0:n].unsqueeze(2).broadcast_to([P, n, HD]), ALU.mult))
                ve.sem_inc(qs_free if q else ks_free, 1)
                then(ve.tensor_tensor(y2, y1, g_all, ALU.mult))
                if t == 0 and q:
                    ve.wait_ge(rope_in, b * 16 + 16)
                then(ve.tensor_tensor(y1, y2, cos, ALU.mult), False)
                half = HD // 2
                o1 = dst[:, t % 2, :].rearrange("p (h c d) -> p h c d", h=n, c=2)
                ve.wait_ge((qo_out if q else ko_out)[t % 2], b * 32 + 16 * (t // 2 + 1))
                then(ve.tensor_tensor(o1[:, :, 1, 0:half], y2[:, :, half:HD],
                                      sin[:, :, 0:half].broadcast_to([P, n, half]), ALU.mult), False)
                then(ve.tensor_tensor(o1[:, :, 1, half:HD], y2[:, :, 0:half],
                                      sin[:, :, half:HD].broadcast_to([P, n, half]), ALU.mult))
                then(ve.tensor_tensor(o1[:, :, 0, :], y1, o1[:, :, 1, :], ALU.add))
                ve.tensor_copy(o1[:, :, 1, :], o1[:, :, 0, :]).then_inc(qo_ready if q else ko_ready, 1)

            ve.wait_ge(const_in, 80)
            normed(0, 0)
            for t in range(TT):
                if t < TT - 1:
                    normed(0, t + 1)
                lo_part(0, t, 0)
            with ve.Fori(0, NBLK // 2) as it:
                for u in range(2):
                    b = it * 2 + u
                    for i in range(NCH):
                        g = GROUP_OF[i]
                        for t in NORM_AT.get(i, ()):
                            normed(b + 1, t)
                        heads_at = g <= 1 and GROUP_OF[i + 1] != g
                        if heads_at:
                            for t in range(TT):
                                head_squares(it, u, t, g == 0)
                        if i % 2 == 1:
                            lo_part(b + 1, i // 2, 1 - u)
                        if heads_at:
                            for t in range(TT):
                                rotated(it, u, t, g == 0)


def mixer_a_phase(nc, ident_d, fold_d, scr):
    NT = S // P
    G = NHA // NKV
    NC = 2 * G
    NR = 4
    with ExitStack() as ctx:
        k = Kit(nc, ctx, "mixa")
        ident = k.sb("ident", [P, P])
        fold = k.sb("fold", [P, HD])
        k_raw = k.sb("k_raw", [P, NT, NKV * 2 * HD])
        v_raw = k.sb("v_raw", [P, NT, NKV * HD])
        kT = [[k.sb(f"kT{g}{h}", [P, S], F32R) for h in range(2)] for g in range(NKV)]
        v_hl = k.sb("v_hl", [P, NT, NKV, 2 * HD], F32R)
        q_in = k.sb("q_in", [P, NHA * 2 * HD])
        qT = [k.sb(f"qT{g}", [P, G, P], F32R) for g in range(NKV)]
        prob = [k.sb(f"prob{u}", [P, G, S]) for u in range(2)]
        pT = [k.sb(f"pT{h}", [P, NR, BANK], F32R) for h in range(2)]
        oT = k.sb("oT", [P, 2, BANK])
        y_half = k.sb("y_half", [P, 2, G * HD])
        y_st = k.sb("y_st", [P, 2, G * HD])
        nmax = k.sb("nmax", [P, 2, 2, G])
        nrow = k.sb("nrow", [P, G])
        below = k.sb("below", [P, 2, G])
        scale = k.sb("scale", [P, 2, 2, G])
        den = k.sb("den", [P, 2, 2, G])
        dscaled = k.sb("dscaled", [P, 2, G])
        dsum = k.sb("dsum", [P, G])
        rden = k.sb("rden", [P, G])
        factor = k.sb("factor", [P, 2, 2, G])
        score = ctx.enter_context(nc.psum_tensor("mixa_score", [P, 4 * BANK], F32))
        turned = [ctx.enter_context(nc.psum_tensor(f"mixa_turned{i}", [P, BANK], F32)) for i in range(2)]
        out_acc = [ctx.enter_context(nc.psum_tensor(f"mixa_out_acc{i}", [P, BANK], F32)) for i in range(2)]
        turn_banks = [turned[0][:], turned[1][:]] + [score[:, i * BANK:(i + 1) * BANK] for i in range(4)]

        const_in, kv_in, q_dma = k.sem("const_in"), k.sem("kv_in"), k.sem("q_dma")
        kt_done, kt_hi, kt_lo = k.sem("kt_done"), k.sem("kt_hi"), k.sem("kt_lo")
        v_hi, v_lo = k.sem("v_hi"), k.sem("v_lo")
        qt_done, qt_hi, qt_lo = k.sem("qt_done"), k.sem("qt_hi"), k.sem("qt_lo")
        sc_done, nm_done, exp_done = (k.sem(n) for n in ("sc_done", "nm_done", "exp_done"))
        t_done, hi_done, lo_done, pv_done = (k.sem(n) for n in ("t_done", "hi_done", "lo_done", "pv_done"))
        row_done, merge, scale_done, recip_done = k.sem("row_done"), k.sem("merge"), k.sem("scale_done"), k.sem("recip_done")
        o_done, fold_done, half_done, y_done = (k.sem(n) for n in ("o_done", "fold_done", "half_done", "y_done"))
        y_out = k.sems("y_out", 2)
        rows_out = k.sem("rows_out")
        set_done = k.sem("set_done")
        MERGE = 4
        block = ctx.enter_context(nc.Block())


        @block.sync
        def _(sp):
            sp.dma_start(ident[:], ident_d).then_inc(const_in, 16)
            sp.dma_start(fold[:], fold_d).then_inc(const_in, 16)
            sp.dma_start(q_in[:], scr["qA"][0:P, :]).then_inc(q_dma, 16)
            sp.dma_start(k_raw[:], scr["kA"].rearrange("(j p) c -> p j c", p=P)).then_inc(kv_in, 16)
            sp.dma_start(v_raw[:], scr["vA"].rearrange("(j p) c -> p j c", p=P)).then_inc(kv_in, 16)
            sp.wait_ge(qt_done, 2)
            sp.dma_start(q_in[:], scr["qA"][P:2 * P, :]).then_inc(q_dma, 16)

            def store(g, row, count):
                sp.wait_ge(y_done, count)
                sp.dma_start(scr["yA"][row, g * G * HD:(g + 1) * G * HD], y_st[:, g, :]).then_inc(y_out[g], 16)

            def one(it, tile):
                store(1, bass.ds(it * P, P), it * 2 + 1)
                store(0, bass.ds(it * P + P, P), it * 2 + 2)
                sp.wait_ge(qt_done, it * 2 + 4)
                sp.dma_start(q_in[:], scr["qA"][tile, :]).then_inc(q_dma, 16)

            def bias_rows(h):
                a, to = scr["bias"][bass.ds(h, 1), :], scr["table"][bass.ds(h, 1), :, :].rearrange("h p n -> (h p) n")
                sp.dma_start(to[:, 0:OWN_W + P], bass.AP(a.tensor, a.offset + 7 * VL, [[0, P], [1, OWN_W + P]])
                             ).then_inc(rows_out, 16)
                sp.dma_start(to[:, OWN_W + P:ROWS_W].rearrange("p (v n) -> p v n", v=7),
                             bass.AP(a.tensor, a.offset + BANK - PAD - P, [[0, P], [VL, 7], [1, P + 2 * PAD + P]])
                             ).then_inc(rows_out, 16)

            with sp.Fori(0, NHB) as it:
                one(it, bass.ds(it * P + 2 * P, P))
                bias_rows(it)
            with sp.Fori(NHB, NT - 2) as it:
                one(it, bass.ds(it * P + 2 * P, P))
            one(NT - 2, slice(0, P))
            one(NT - 1, slice(0, P))
            store(1, slice(NT * P, NT * P + P), 2 * NT + 1)
            sp.wait_ge(rows_out, 32 * NHB)
            sp.wait_ge(y_out[0], 16 * (NT + 1))
            sp.wait_ge(y_out[1], 16 * (NT + 2))
            sp.wait_ge(q_dma, 16 * (NT + 2))

        @block.gpsimd
        def _(pool):
            pool.memset(pT[0][:, 2:4, :].bitcast(F32), 0.0).then_inc(set_done, 1)
            pool.memset(pT[1][:, 2:4, :].bitcast(F32), 0.0).then_inc(set_done, 1)
            pool.memset(factor[:], 0.0).then_inc(set_done, 1)
            pool.memset(y_half[:], 0.0).then_inc(set_done, 1)
            pool.sem_inc(pv_done, 2)
            pool.sem_inc(lo_done, 2)
            pool.sem_inc(half_done, 1)
            for s in y_out:
                pool.sem_inc(s, 16)

            def merged(U, w):
                pool.wait_ge(exp_done, U * NC + NC)
                pool.wait_ge(row_done, U + 1)
                pool.tensor_tensor(below[:], nrow[:].unsqueeze(1).broadcast_to([P, 2, G]), nmax[:, w, :, :],
                                   ALU.subtract).then_inc(merge, 1)
                pool.wait_ge(scale_done, U + 1)
                pool.tensor_tensor(dscaled[:], den[:, w, :, :], scale[:, w, :, :], ALU.mult).then_inc(merge, 1)
                pool.wait_ge(merge, U * MERGE + 2)
                pool.tensor_tensor(dsum[:], dscaled[:, 0, :], dscaled[:, 1, :], ALU.add).then_inc(merge, 1)
                pool.wait_ge(recip_done, U + 1)
                pool.tensor_tensor(factor[:, w, :, :], scale[:, w, :, :], rden[:].unsqueeze(1).broadcast_to([P, 2, G]),
                                   ALU.mult).then_inc(merge, 1)

            def summed(count, slot, stored):
                pool.wait_ge(half_done, count * 2)
                pool.wait_ge(y_out[slot], stored)
                pool.tensor_tensor(y_st[:, slot, :], y_half[:, 0, :], y_half[:, 1, :], ALU.add).then_inc(y_done, 1)

            with pool.Fori(0, NT) as it:
                for w in range(2):
                    U = it * 2 + w
                    merged(U, w)
                    summed(U + 1, 1 - w, it * 16 + 16)
            summed(2 * NT + 1, 1, 16 * NT + 16)

        @block.tensor
        def _(pe):
            def turn_queries(V, g, bank, first=False):
                pe.wait_ge(q_dma, (V - g) * 8 + 16)
                if not first:
                    pe.wait_ge(half_done, V * 2 - 2)
                for h in range(G):
                    mm = pe.transpose(bank[:, h * P:(h + 1) * P], q_in[:, (G * g + h) * P:(G * g + h + 1) * P], ident[:])
                mm.then_inc(qt_done, 1)

            def scores(V, g, c):
                half, h = c // G, c % G
                if c == 0:
                    pe.wait_ge(qt_lo, V + 1)
                if not (isinstance(V, int) and c < 2):
                    pe.wait_ge(exp_done, V * NC + c - 1)
                for j in range(2):
                    kc = 2 * half + j
                    at = 2 * (c % 2) + j
                    for part in range(2):
                        mm = pe.matmul(score[:, at * BANK:(at + 1) * BANK], qT[g][:, h, :],
                                       kT[g][part][:, kc * BANK:(kc + 1) * BANK], start=part == 0, stop=part == 1)
                mm.then_inc(sc_done, 1)

            def values(U, g, s):
                half = s // (NT // 2)
                pe.wait_ge(lo_done, U * NT + s + 3)
                if s == 0:
                    pe.wait_ge(half_done, U * 2 + 1)
                if s == NT // 2:
                    pe.wait_ge(qt_lo, U + 3)
                for part in range(2):
                    mm = pe.matmul(out_acc[half][:], v_hl[:, s, g, :], pT[part][:, s % NR, :],
                                   start=s % (NT // 2) == 0 and part == 0,
                                   stop=s % (NT // 2) == NT // 2 - 1 and part == 1)
                mm.then_inc(pv_done, 1)

            def fold_out(count, half):
                pe.wait_ge(o_done, count)
                for h in range(G):
                    mm = pe.matmul(out_acc[half][:, h * HD:(h + 1) * HD], oT[:, half, h * P:(h + 1) * P], fold[:],
                                   start=True, stop=True)
                mm.then_inc(fold_done, 1)

            pe.wait_ge(const_in, 32)
            pe.wait_ge(q_dma, 16)
            turn_queries(0, 0, out_acc[0], True)
            turn_queries(1, 1, out_acc[1], True)
            pe.wait_ge(kv_in, 32)
            for n in range(2 * NT // 4):
                g, j0 = n // 4, 4 * (n % 4)
                if n >= 6:
                    pe.wait_ge(kt_lo, n - 5)
                for j in range(4):
                    mm = pe.transpose(turn_banks[n % 6][:, j * P:(j + 1) * P], k_raw[:, j0 + j, g * P:(g + 1) * P],
                                      ident[:])
                mm.then_inc(kt_done, 1)
            pe.wait_ge(kt_lo, 6)
            for c in range(NC):
                scores(0, 0, c)
            pe.wait_ge(kt_lo, 2 * NT // 4)
            pe.wait_ge(v_lo, 1)
            pe.wait_ge(set_done, 4)
            pe.wait_ge(qt_lo, 2)
            pe.matmul(out_acc[1][:], v_hl[:, NT - 3, 1, :], pT[0][:, 2, :], start=True, stop=False)
            with pe.Fori(0, NT) as it:
                for w in range(2):
                    U = it * 2 + w
                    for s in range(NT):
                        if s in (0, NT // 2):
                            pe.wait_ge(exp_done, U * NC + (G if s == 0 else NC))
                        pe.wait_ge(lo_done, U * NT + s + 1)
                        for h in range(G):
                            mm = pe.transpose(turned[s % 2][:, h * P:(h + 1) * P], prob[w][:, h, s * P:(s + 1) * P],
                                              ident[:])
                        mm.then_inc(t_done, 1)
                        if s < 2:
                            values(U - 1, 1 - w, s + NT - 2)
                        else:
                            values(U, w, s - 2)
                        if s % 2 == 0:
                            scores(U + 1, 1 - w, s // 2)
                        if s == 4:
                            fold_out(U * 2 + 1, 1)
                        if s == 6:
                            turn_queries(U + 2, w, out_acc[1])
                        if s == 12:
                            fold_out(U * 2 + 2, 0)
            values(2 * NT - 1, 1, NT - 2)
            values(2 * NT - 1, 1, NT - 1)
            fold_out(4 * NT + 1, 1)

        @block.scalar
        def _(act):
            def query_hi(V, g, bank):
                act.wait_ge(qt_done, V + 1)
                act.activation(qT[g][:].rearrange("p h n -> p (h n)"), bank[:], ACT.Copy).then_inc(qt_hi, 1)

            def exponential(V, par, c):
                half, h = c // G, c % G
                act.wait_ge(nm_done, V * NC + c + 1)
                act.activation(prob[par][:, h, half * 2 * BANK:(half + 1) * 2 * BANK],
                               score[:, 2 * (c % 2) * BANK:2 * (c % 2 + 1) * BANK], ACT.Exp,
                               bias=nmax[:, par, half, h:h + 1], accum_out=den[:, par, half, h:h + 1]
                               ).then_inc(exp_done, 1)

            def sums_out(U, half):
                act.wait_ge(pv_done, U * NT + (half + 1) * NT // 2 + 4)
                act.activation(oT[:, half, :], out_acc[half][:], ACT.Copy).then_inc(o_done, 1)

            query_hi(0, 0, out_acc[0])
            query_hi(1, 1, out_acc[1])
            act.wait_ge(kv_in, 32)
            for n in range(2 * NT // 4):
                act.wait_ge(kt_done, n + 1)
                act.activation(kT[n // 4][0][:, (n % 4) * BANK:(n % 4 + 1) * BANK], turn_banks[n % 6], ACT.Copy
                               ).then_inc(kt_hi, 1)
            act.activation(v_hl[:, :, :, 0:HD], v_raw[:].rearrange("p j (g d) -> p j g d", g=NKV), ACT.Copy
                           ).then_inc(v_hi, 1)
            for c in range(NC - 1):
                exponential(0, 0, c)
            with act.Fori(0, NT) as it:
                for w in range(2):
                    U = it * 2 + w
                    for s in range(NT):
                        act.wait_ge(t_done, U * NT + s + 1)
                        act.wait_ge(pv_done, U * NT + s + 1)
                        act.activation(pT[0][:, s % NR, :], turned[s % 2][:], ACT.Copy).then_inc(hi_done, 1)
                        if s == 0:
                            exponential(U, w, NC - 1)
                        elif s % 2 == 0:
                            exponential(U + 1, 1 - w, s // 2 - 1)
                        if s == 3:
                            sums_out(U - 1, 1)
                            act.wait_ge(merge, U * MERGE + 1)
                            act.activation(scale[:, w, :, :], below[:], ACT.Exp).then_inc(scale_done, 1)
                        if s == 7:
                            query_hi(U + 2, w, out_acc[1])
                        if s == 11:
                            sums_out(U, 0)
            sums_out(2 * NT - 1, 1)

        @block.vector
        def _(ve):
            def query_lo(V, g, bank):
                ve.wait_ge(qt_hi, V + 1)
                lower = qT[g][HD:P, :, :].rearrange("p h n -> p (h n)")
                ve.tensor_tensor(lower, bank[HD:P, :], lower.bitcast(F32), ALU.subtract).then_inc(qt_lo, 1)

            def maximum(V, par, c):
                ve.wait_ge(sc_done, V * NC + c + 1)
                ve.tensor_reduce(nmax[:, par, c // G, c % G:c % G + 1], score[:, 2 * (c % 2) * BANK:
                                                                             2 * (c % 2 + 1) * BANK],
                                 AXX, ALU.max, negate=True).then_inc(nm_done, 1)

            def output(count, slot, half):
                ve.wait_ge(fold_done, count)
                ve.tensor_tensor(y_half[:, half, :].rearrange("p (h d) -> p h d", h=G),
                                 out_acc[half][:, 0:G * HD].rearrange("p (h d) -> p h d", h=G),
                                 factor[:, slot, half, :].unsqueeze(2).broadcast_to([P, G, HD]), ALU.mult
                                 ).then_inc(half_done, 1)

            query_lo(0, 0, out_acc[0])
            query_lo(1, 1, out_acc[1])
            for n in range(2 * NT // 4):
                at = slice((n % 4) * BANK, (n % 4 + 1) * BANK)
                ve.wait_ge(kt_hi, n + 1)
                ve.tensor_tensor(kT[n // 4][1][:, at], turn_banks[n % 6], kT[n // 4][0][:, at].bitcast(F32),
                                 ALU.subtract).then_inc(kt_lo, 1)
            ve.wait_ge(v_hi, 1)
            ve.tensor_tensor(v_hl[:, :, :, HD:2 * HD], v_raw[:].rearrange("p j (g d) -> p j g d", g=NKV),
                             v_hl[:, :, :, 0:HD].bitcast(F32), ALU.subtract).then_inc(v_lo, 1)
            for c in range(NC):
                maximum(0, 0, c)
            with ve.Fori(0, NT) as it:
                for w in range(2):
                    U = it * 2 + w
                    for s in range(NT):
                        ve.wait_ge(hi_done, U * NT + s + 1)
                        ve.tensor_tensor(pT[1][:, s % NR, :], turned[s % 2][:], pT[0][:, s % NR, :].bitcast(F32),
                                         ALU.subtract).then_inc(lo_done, 1)
                        if s % 2 == 0:
                            maximum(U + 1, 1 - w, s // 2)
                        if s == 1:
                            ve.wait_ge(nm_done, U * NC + NC)
                            ve.tensor_tensor(nrow[:], nmax[:, w, 0, :], nmax[:, w, 1, :], ALU.min).then_inc(row_done, 1)
                        if s == 5:
                            output(U * 2 + 1, 1 - w, 1)
                            ve.wait_ge(merge, U * MERGE + 3)
                            ve.reciprocal(rden[:], dsum[:]).then_inc(recip_done, 1)
                        if s == 7:
                            query_lo(U + 2, w, out_acc[1])
                        if s == 13:
                            ve.wait_ge(merge, U * MERGE + 4)
                            ve.wait_ge(y_done, U + 1)
                            output(U * 2 + 2, w, 0)
            output(4 * NT + 1, 1, 1)


def mixer_b_phase(nc, ident_d, fold_d, scr):
    NU = 16
    NK = 8
    VT = NU + RES
    SW = S + 2 * PAD
    SLOTS = 4
    with ExitStack() as ctx:
        k = Kit(nc, ctx, "mixb")
        ident = k.sb("ident", [P, P])
        fold = k.sb("fold", [P, HD])
        q_in = k.sb("q_in", [P, NU, 2 * HD])
        k_in = k.sb("k_in", [P, NU, 2 * HD])
        v_in = k.sb("v_in", [P, VT, HD])
        kT = [[k.sb(f"kT{u}{h}", [P, SW], F32R) for h in range(2)] for u in range(2)]
        qT = [k.sb(f"qT{u}", [P, S], F32R) for u in range(2)]
        v_hl = [k.sb(f"v_hl{u}", [P, VT, 2 * HD], F32R) for u in range(2)]
        t_own = [k.sb(f"t_own{u}", [P, 7 * P]) for u in range(2)]
        t_oth = [k.sb(f"t_oth{u}", [P, 6, P]) for u in range(2)]
        t_near = k.sb("t_near", [P, TABLE_W - OWN_W])
        t_end = [k.sb(f"t_end{u}", [P, 3, RES, RES, 2, PAD]) for u in range(2)]
        prob = k.sb("prob", [P, SLOTS, 2 * BANK])
        pT = k.sb("pT", [P, 2, NK, 2, P], F32R)
        pmax = k.sb("pmax", [P, SLOTS, 3])
        nmax = k.sb("nmax", [P, SLOTS])
        den = k.sb("den", [P, SLOTS])
        rden = k.sb("rden", [P, SLOTS])
        oT = k.sb("oT", [P, 2, 2 * P])
        y_st = k.sb("y_st", [P, 2, NU, HD])
        score = [ctx.enter_context(nc.psum_tensor(f"mixb_score{i}", [P, 2 * BANK], F32)) for i in range(2)]
        turned = [ctx.enter_context(nc.psum_tensor(f"mixb_turned{i}", [P, BANK], F32)) for i in range(2)]
        out_acc = ctx.enter_context(nc.psum_tensor("mixb_out_acc", [P, BANK], F32))
        prep = ctx.enter_context(nc.psum_tensor("mixb_prep", [P, BANK], F32))

        const_in, set_done = k.sem("const_in"), k.sem("set_done")
        qk_dma, v_dma, t_dma = k.sem("qk_dma"), k.sem("v_dma"), k.sem("t_dma")
        t_done_pool, pool_step = k.sem("t_done_pool"), k.sem("pool_step")
        ve_step = k.sem("ve_step")
        pre_done, pre_hi, pre_lo, v_hi, v_lo = (k.sem(n) for n in ("pre_done", "pre_hi", "pre_lo", "v_hi", "v_lo"))
        sc_done, add_done, nm_done, exp_done = (k.sem(n) for n in ("sc_done", "add_done", "nm_done", "exp_done"))
        t_done, hi_done, lo_done, pv_done = (k.sem(n) for n in ("t_done", "hi_done", "lo_done", "pv_done"))
        rd_done, o_done, fold_done, y_done = (k.sem(n) for n in ("rd_done", "o_done", "fold_done", "y_done"))
        y_out = k.sems("y_out", 2)
        QK_DMAS, V_DMAS = 2, 1 + 2 * RES
        T_COPIES = 2 + 3 * RES
        PRE = 8
        block = ctx.enter_context(nc.Block())

        @block.sync
        def _(sp):
            def copies(name, h):
                a = scr[name][:, bass.ds(h * 2 * HD, 2 * HD)]
                return bass.AP(a.tensor, a.offset, [[2 * D_AB, P], [2 * P * D_AB, NU], [1, 2 * HD]])

            def load_qk(h):
                sp.dma_start(q_in[:], copies("qB", h)).then_inc(qk_dma, 16)
                sp.dma_start(k_in[:], copies("kB", h)).then_inc(qk_dma, 16)

            def load_v(h):
                sp.dma_start(v_in[:, 0:NU, :], scr["vB"][PAD:PAD + S, bass.ds(h * HD, HD)].rearrange(
                    "(j p) c -> p j c", p=P)).then_inc(v_dma, 16)
                for r in range(RES):
                    for side in range(2):
                        row = r * SUB + side * (P + PAD)
                        a = scr["vB"][row:row + PAD, bass.ds(h * HD, HD)]
                        sp.dma_start(v_in[(2 * r + side) * PAD:(2 * r + side + 1) * PAD, NU:VT, :],
                                     bass.AP(a.tensor, a.offset, [[D_AB, PAD], [P * D_AB, RES], [1, HD]])
                                     ).then_inc(v_dma, 16)

            def load_tables(h, par):
                a = scr["table"][bass.ds(h, 1), :, :]
                sp.dma_start(t_own[par][:], bass.AP(a.tensor, a.offset + P - 1, [[ROWS_W - 1, P], [1, OWN_W]])
                             ).then_inc(t_dma, 16)
                sp.dma_start(t_near[:].rearrange("p (v n) -> p v n", v=7),
                             bass.AP(a.tensor, a.offset + OWN_W + 2 * P - 1,
                                     [[ROWS_W - 1, P], [P + 2 * PAD + P, 7], [1, P + 2 * PAD]])).then_inc(t_dma, 16)

            sp.dma_start(ident[:], ident_d).then_inc(const_in, 16)
            load_qk(0)
            sp.dma_start(fold[:], fold_d).then_inc(const_in, 16)
            load_v(0)
            load_tables(0, 0)

            def load_next(h, nxt):
                sp.wait_ge(pre_done, h * PRE + PRE)
                load_qk(nxt)
                sp.wait_ge(v_lo, h + 1)
                load_v(nxt)

            def next_tables(h, par, nxt):
                sp.wait_ge(add_done, h * (3 * NU) + 6)
                sp.wait_ge(t_done_pool, h * T_COPIES + T_COPIES)
                load_tables(nxt, 1 - par)

            def store(h, par):
                sp.wait_ge(y_done, h * NU + NU + 1)
                a = scr["yB"][:, bass.ds(h * HD, HD)]
                sp.dma_start(bass.AP(a.tensor, a.offset, [[D_AB, P], [P * D_AB, NU], [1, HD]]), y_st[:, par, :, :]
                             ).then_inc(y_out[par], 16)

            def one(h, par, nxt):
                load_next(h, nxt)
                next_tables(h, par, nxt)
                store(h - 1, 1 - par)

            load_next(0, 1)
            next_tables(0, 0, 1)
            with sp.Fori(0, NHB // 2 - 1) as it:
                for u in range(2):
                    one(it * 2 + 1 + u, 1 - u, it * 2 + 2 + u)
            one(NHB - 1, 1, 0)
            store(NHB - 1, 1)
            for s in y_out:
                sp.wait_ge(s, 16 * (NHB // 2 + 1))
            sp.wait_ge(t_dma, 32 * (NHB + 1))
            sp.wait_ge(qk_dma, 16 * QK_DMAS * (NHB + 1))
            sp.wait_ge(v_dma, 16 * V_DMAS * (NHB + 1))

        @block.gpsimd
        def _(pool):
            for u in range(2):
                for h in range(2):
                    pool.memset(kT[u][h][:, 0:PAD].bitcast(F32), 0.0)
                    pool.memset(kT[u][h][:, PAD + S:SW].bitcast(F32), 0.0).then_inc(set_done, 1)
                pool.memset(t_end[u][:], NEG).then_inc(set_done, 1)
            for s in y_out:
                pool.sem_inc(s, 16)
            pool.memset(oT[:, 1, :], 0.0).then_inc(set_done, 1)
            pool.memset(rden[:, SLOTS - 1:SLOTS], 0.0).then_inc(set_done, 1)
            pool.sem_inc(o_done, 1)

            def tables(par):
                near = t_near[:].rearrange("p (v n) -> p v n", v=7)
                for i, v in enumerate((0, 4)):
                    pool.tensor_copy(t_oth[par][:, 3 * i:3 * i + 3, :], near[:, v:v + 3, PAD:PAD + P]
                                     ).then_inc(t_done_pool, 1)
                for r in range(RES):
                    a = near[:, 3 - r:7 - r, 0:PAD]
                    both = bass.AP(a.tensor, a.offset, [[TABLE_W - OWN_W, P], [P + 2 * PAD, RES], [P + PAD, 2],
                                                        [1, PAD]])
                    pool.tensor_copy(t_end[par][:, 1, r, :, :, :], both).then_inc(t_done_pool, 1)
                    pool.tensor_copy(t_end[par][:, 0, r, :, 1, :], near[:, 3 - r:7 - r, PAD + P:2 * PAD + P]
                                     ).then_inc(t_done_pool, 1)
                    pool.tensor_copy(t_end[par][:, 2, r, :, 0, :], near[:, 3 - r:7 - r, 0:PAD]
                                     ).then_inc(t_done_pool, 1)

            pool.wait_ge(set_done, 8)
            pool.wait_ge(t_dma, 32)
            tables(0)
            with pool.Fori(0, NHB // 2) as it:
                for par in range(2):
                    h = it * 2 + par
                    pool.wait_ge(t_dma, h * 32 + 64)
                    pool.wait_ge(add_done, h * (3 * NU) + 6)
                    pool.sem_inc(pool_step, 1)
                    tables(1 - par)

        def others(r):
            return [x for x in range(RES) if x != r]

        @block.tensor
        def _(pe):
            def prepare(h, m):
                if m == 0:
                    pe.wait_ge(qk_dma, h * (16 * QK_DMAS) + 16 * QK_DMAS)
                if not (isinstance(h, int) and m == 0):
                    pe.wait_ge(pre_lo, h * PRE + m)
                src = q_in if m < 4 else k_in
                for j in range(4):
                    mm = pe.transpose(prep[:, j * P:(j + 1) * P],
                                      src[:, 4 * (m % 4) + j, :], ident[:])
                mm.then_inc(pre_done, 1)

            def scores(N, par, n):
                r, b = n // RES, n % RES
                if not (isinstance(N, int) and N < 2):
                    pe.wait_ge(add_done, N * 3 - 3)
                sc = score[n % 2]
                q = qT[par][:, n * P:(n + 1) * P]
                for part in range(2):
                    kt = kT[par][part]
                    main = kt[:, PAD:PAD + S].rearrange("p (r m) -> p r m", r=RES)
                    pe.matmul(sc[:, 0:BANK], q, main[:, r, :], start=part == 0, stop=part == 1)
                at = BANK
                runs = [x for x in ((0, r), (r + 1, RES)) if x[1] > x[0]]
                for a, z in runs:
                    for part in range(2):
                        main = kT[par][part][:, PAD:PAD + S].rearrange("p (r m) -> p r m", r=RES)
                        pe.matmul(sc[:, at:at + (z - a) * P], q, main[:, a:z, b * P:(b + 1) * P],
                                  start=part == 0, stop=part == 1)
                    at += (z - a) * P
                for part in range(2):
                    t = kT[par][part][:, b * P:b * P + PAD]
                    ends = bass.AP(t.tensor, t.offset, [[SW, P], [SUB, RES], [P + PAD, 2], [1, PAD]])
                    mm = pe.matmul(sc[:, at:at + P], q, ends, start=part == 0, stop=part == 1)
                mm.then_inc(sc_done, 1)

            def turn(N, n):
                pe.wait_ge(exp_done, N + 1)
                for half in range(2):
                    if not (isinstance(N, int) and N == 0):
                        pe.wait_ge(lo_done, N * 2 + half - 1)
                    for j in range(4):
                        c = 4 * half + j
                        mm = pe.transpose(turned[half][:, j * P:(j + 1) * P], prob[:, n % SLOTS, c * P:(c + 1) * P],
                                          ident[:])
                    mm.then_inc(t_done, 1)

            def values(N, par, n):
                r, b = n // RES, n % RES
                tiles = [RES * r + j for j in range(4)] + [RES * x + b for x in others(r)] + [NU + b]
                pe.wait_ge(lo_done, N * 2 + 2)
                pe.wait_ge(y_done, N + 1)
                for c, vt in enumerate(tiles):
                    mm = pe.matmul(out_acc[:, 0:2 * P], v_hl[par][:, vt, :],
                                   pT[:, n % 2, c, :, :].rearrange("p h n -> p (h n)"), start=c == 0, stop=c == NK - 1)
                mm.then_inc(pv_done, 1)

            def fold_out(count, n):
                pe.wait_ge(o_done, count)
                for part in range(2):
                    mm = pe.matmul(out_acc[:, 0:HD], oT[:, n % 2, part * P:(part + 1) * P], fold[:],
                                   start=part == 0, stop=part == 1)
                mm.then_inc(fold_done, 1)

            pe.wait_ge(const_in, 32)
            for m in range(PRE):
                prepare(0, m)
            pe.wait_ge(set_done, 8)
            pe.wait_ge(pre_lo, PRE)
            scores(0, 0, 0)
            scores(1, 0, 1)
            pe.wait_ge(v_lo, 1)
            turn(0, 0)
            with pe.Fori(0, NHB // 2) as it:
                for par in range(2):
                    h = it * 2 + par
                    for n in range(NU):
                        N = h * NU + n
                        if n < NU - 2:
                            scores(N + 2, par, n + 2)
                        else:
                            if n == NU - 2:
                                pe.wait_ge(pre_lo, h * PRE + 2 * PRE)
                                pe.wait_ge(v_lo, h + 2)
                            scores(N + 2, 1 - par, n + 2 - NU)
                        fold_out(N + 1, n - 1)
                        turn(N + 1, (n + 1) % NU)
                        values(N, par, n)
                        if 2 <= n < 2 + PRE:
                            prepare(h + 1, n - 2)
            fold_out(NHB * NU + 1, NU - 1)

        @block.scalar
        def _(act):
            def pre_hi_part(h, par, m):
                act.wait_ge(pre_done, h * PRE + m + 1)
                dst = qT[par][:, m * BANK:(m + 1) * BANK] if m < 4 else kT[par][0][:, PAD + (m - 4) * BANK:
                                                                               PAD + (m - 3) * BANK]
                act.activation(dst, prep[:], ACT.Copy).then_inc(pre_hi, 1)

            def value_hi(h, par):
                act.wait_ge(v_dma, h * (16 * V_DMAS) + 16 * V_DMAS)
                act.activation(v_hl[par][:, :, 0:HD], v_in[:], ACT.Copy).then_inc(v_hi, 1)

            def exponential(N, n):
                act.wait_ge(nm_done, N + 1)
                p = prob[:, n % SLOTS, :]
                act.activation(p, p, ACT.Exp, bias=nmax[:, n % SLOTS:n % SLOTS + 1],
                               accum_out=den[:, n % SLOTS:n % SLOTS + 1]).then_inc(exp_done, 1)

            def turned_hi(N, n):
                for half in range(2):
                    act.wait_ge(t_done, N * 2 + half + 1)
                    act.activation(pT[:, n % 2, 4 * half:4 * half + 4, 0, :],
                                   turned[half][:].rearrange("p (c n) -> p c n", c=4), ACT.Copy).then_inc(hi_done, 1)

            def sums_out(N, n):
                act.wait_ge(pv_done, N + 1)
                act.activation(oT[:, n % 2, :], out_acc[:, 0:2 * P], ACT.Copy).then_inc(o_done, 1)

            for m in range(PRE):
                pre_hi_part(0, 0, m)
            value_hi(0, 0)
            exponential(0, 0)
            exponential(1, 1)
            turned_hi(0, 0)
            with act.Fori(0, NHB // 2) as it:
                for par in range(2):
                    h = it * 2 + par
                    for n in range(NU):
                        N = h * NU + n
                        turned_hi(N + 1, n + 1)
                        sums_out(N, n)
                        exponential(N + 2, n + 2)
                        if 2 <= n < 2 + PRE:
                            pre_hi_part(h + 1, 1 - par, n - 2)
                        if n == 10:
                            value_hi(h + 1, 1 - par)

        @block.vector
        def _(ve):
            def pre_lo_part(h, par, m):
                ve.wait_ge(pre_hi, h * PRE + m + 1)
                if m < 4:
                    at = slice(m * BANK, (m + 1) * BANK)
                    low = qT[par][HD:P, at]
                    ve.tensor_tensor(low, prep[HD:P, :], low.bitcast(F32), ALU.subtract).then_inc(pre_lo, 1)
                else:
                    at = slice(PAD + (m - 4) * BANK, PAD + (m - 3) * BANK)
                    ve.tensor_tensor(kT[par][1][:, at], prep[:], kT[par][0][:, at].bitcast(F32), ALU.subtract
                                     ).then_inc(pre_lo, 1)

            def value_lo(h, par):
                ve.wait_ge(v_hi, h + 1)
                ve.tensor_tensor(v_hl[par][:, :, HD:2 * HD], v_in[:], v_hl[par][:, :, 0:HD].bitcast(F32), ALU.subtract
                                 ).then_inc(v_lo, 1)

            def add_bias(N, par, n):
                r, b = n // RES, n % RES
                edge = 0 if b == 0 else 2 if b == RES - 1 else 1
                sc, slot = score[n % 2], n % SLOTS
                parts = ((0, BANK, t_own[par][:, (3 - b) * P:(7 - b) * P]),
                         (BANK, BANK + 3 * P, t_oth[par][:, 3 - r:6 - r, :].rearrange("p a n -> p (a n)")),
                         (BANK + 3 * P, 2 * BANK, t_end[par][:, edge, r, :, :, :].rearrange("p a s n -> p (a s n)")))
                ve.wait_ge(sc_done, N + 1)
                ve.sem_inc(ve_step, 1)
                for i, (a, z, table) in enumerate(parts):
                    ve.tensor_tensor_reduce(prob[:, slot, a:z], sc[:, a:z], table, 1.0, -3.0e38, ALU.add, ALU.max,
                                            pmax[:, slot, i:i + 1]).then_inc(add_done, 1)
                ve.wait_ge(add_done, N * 3 + 3)
                ve.tensor_reduce(nmax[:, slot:slot + 1], pmax[:, slot, :], AXX, ALU.max, negate=True).then_inc(nm_done, 1)

            def turned_lo(N, n):
                for half in range(2):
                    at = pT[:, n % 2, 4 * half:4 * half + 4, :, :]
                    ve.wait_ge(hi_done, N * 2 + half + 1)
                    ve.tensor_tensor(at[:, :, 1, :], turned[half][:].rearrange("p (c n) -> p c n", c=4),
                                     at[:, :, 0, :].bitcast(F32), ALU.subtract).then_inc(lo_done, 1)

            def sums(N, n):
                ve.wait_ge(exp_done, N + 1)
                ve.reciprocal(rden[:, n % SLOTS:n % SLOTS + 1], den[:, n % SLOTS:n % SLOTS + 1]).then_inc(rd_done, 1)

            def output(count, par, n):
                ve.wait_ge(fold_done, count)
                ve.tensor_scalar(y_st[:, par, n, :], out_acc[:, 0:HD], rden[:, n % SLOTS:n % SLOTS + 1], None, ALU.mult
                                 ).then_inc(y_done, 1)

            for m in range(PRE):
                pre_lo_part(0, 0, m)
            value_lo(0, 0)
            ve.wait_ge(t_dma, 32)
            ve.wait_ge(t_done_pool, T_COPIES)
            add_bias(0, 0, 0)
            add_bias(1, 0, 1)
            sums(0, 0)
            turned_lo(0, 0)
            with ve.Fori(0, NHB // 2) as it:
                for par in range(2):
                    h = it * 2 + par
                    for n in range(NU):
                        N = h * NU + n
                        if n == 1:
                            ve.wait_ge(y_out[par], (h - par) * 8 + 16)
                        output(N + 1, par if n else 1 - par, (n - 1) % NU)
                        if n < NU - 2:
                            add_bias(N + 2, par, n + 2)
                        else:
                            if n == NU - 2:
                                ve.wait_ge(t_done_pool, h * T_COPIES + 2 * T_COPIES)
                            add_bias(N + 2, 1 - par, n + 2 - NU)
                        sums(N + 1, n + 1)
                        turned_lo(N + 1, n + 1)
                        if 2 <= n < 2 + PRE:
                            pre_lo_part(h + 1, 1 - par, n - 2)
                        if n == 10:
                            value_lo(h + 1, 1 - par)
            output(NHB * NU + 1, 1, NU - 1)


def feed_phase(nc, x, w_tail, gains, g_out, g_mlp_pre, g_ple, pT_d, ident_d, scr, out):
    CW = 1024
    NR4 = 4
    NF = 8
    GROUPS = D_FF // (NF * P)
    FF = [c for g in range(GROUPS) for c in
          [("f", g, j) for j in range(NF)] + [("g2", g, n, q) for n in range(2) for q in range(4)]]
    G1 = [("g1", 0, n, q) for n in range(2) for q in range(4)]
    G3 = [c for n in range(2) for c in [("g3", 0, n, q) for q in range(4)] + [("ple", 0, n, 0)]]
    NFF, NG1, NCHB = len(FF), len(G1), len(FF) + len(G1) + len(G3)
    LOAD_Y = {4 + 8 * t: t for t in range(TT)}
    NORM_Y = {5 + 8 * t: t for t in range(TT)}
    TURN_Y = {8 + 8 * t: t for t in range(TT)}
    TURN_Z = {2: 0, 3: 1, 4: 2, 5: 3}
    TURN_X = {2: 0, 3: 1, 4: 2, 5: 3}
    SQUARES = ((1, 0), (1, 1), (1, 2), (2, 0), (2, 1), (1, 3), (2, 2), (2, 3))
    P_AT = 48
    with ExitStack() as ctx:
        k = Kit(nc, ctx, "feed")
        ident = k.sb("ident", [P, P])
        gate_in = k.sb("gate_in", [P, 3, KD])
        g_row = k.sb("g_row", [P, 2, D])
        y_in = k.sb("y_in", [P, D])
        xn = k.sb("xn", [P, 2, D])
        junk = k.sb("junk", [P, 2, D], mybir.dt.bfloat16)
        ssq = k.sb("ssq", [P, 12, 2])
        ms = k.sb("ms", [P, 12, 2])
        rec = k.sb("rec", [P, 12, 2])
        rstd = k.sb("rstd", [P, 12, 2])
        xT = [[k.sb(f"xT{u}{h}", [P, KD, BT], F32R) for h in range(2)] for u in range(2)]
        fT = [k.sb(f"fT{h}", [P, NF, BT], F32R) for h in range(2)]
        pT = [k.sb(f"pT{h}", [P, 2, BT], F32R) for h in range(2)]
        w_raw = k.sb("w_raw", [P, NR4, CW])
        w_sp = [k.sb(f"w_split{h}", [P, NSPL, CW], F32R) for h in range(2)]
        total = k.sb("total", [P, TT, D])
        res = k.sb("res", [P, TT, D])
        rl = k.sb("rl", [P, 2, BANK])
        fs = k.sb("fs", [P, 2, BANK])
        bank = k.banks()
        acc, tp, fb = bank[0:4], bank[4:6], bank[6:8]

        const_in = k.sem("const_in")
        w_dma = k.sems("w_dma", NR4)
        w_hi, w_lo, w_used, pool_step = k.sem("w_hi"), k.sem("w_lo"), k.sem("w_used"), k.sem("pool_step")
        sp_step = k.sem("sp_step")
        y_dma, x_dma, h2_out, h2_in, out_dma = (k.sem("y_dma"), k.sems("x_dma", TT), k.sems("h2_out", TT),
                                                k.sems("h2_in", TT), k.sems("out_dma", TT))
        sq_done, var_done, rec_done, rt_done = (k.sem(n) for n in ("sq_done", "var_done", "rec_done", "rt_done"))
        xn_done, tp_done, hi_done, lo_done = (k.sem(n) for n in ("xn_done", "tp_done", "hi_done", "lo_done"))
        acc_done, ev_act, ev_dve = k.sem("acc_done"), k.sem("ev_act"), k.sem("ev_dve")
        f_done, f_relu, f_hi, f_mul, f_lo = (k.sem(n) for n in ("f_done", "f_relu", "f_hi", "f_mul", "f_lo"))
        p_hi, p_lo = k.sem("p_hi"), k.sem("p_lo")
        gained, h_done = k.sem("gained"), k.sem("h_done")
        ple_done, sig_done, prod_done, o_done = (k.sem(n) for n in ("ple_done", "sig_done", "prod_done", "o_done"))
        block = ctx.enter_context(nc.Block())

        norm_at = lambda b: 12 + 20 * b
        turn_at = lambda b: 8 + 12 * b
        acc_at = lambda b: 8 + 48 * b
        act_at = lambda b: 8 + 24 * b
        dve_at = lambda b: 24 * b
        h_at = lambda b: 4 + 8 * b
        f_at = lambda b: 4 * NF * b

        def blocks(eng, body):
            with eng.Fori(0, NBLK // 2) as it:
                for u in range(2):
                    body(it * 2 + u, u)

        @block.sync
        def _(sp):
            def load_y(b, row, t):
                if t > 0:
                    sp.wait_ge(xn_done, t if b is None else turn_at(b) + t)
                elif b is not None:
                    sp.wait_ge(p_lo, b + 1)
                sp.sem_inc(sp_step, 1)
                sp.dma_start(y_in[:, 0:D_AB], scr["yA"][bass.ds(row + (P + t * P), P), :]).then_inc(y_dma, 16)
                sp.dma_start(y_in[:, D_AB:D], scr["yB"][bass.ds(row + t * P, P), :]).then_inc(y_dma, 16)

            def load_w(C, i, slot):
                sp.wait_ge(w_lo, C - NR4 + 1)
                sp.dma_start(w_raw[:, slot, :], w_tail[i]).then_inc(w_dma[slot], 16)

            def load_h2(b, t):
                sp.wait_ge(h_done, h_at(b) + (4 + t + 1))
                sp.wait_ge(h2_out[t], b * 16 + 16)
                sp.dma_start(total[:, t, :], scr["h2"][t * P:(t + 1) * P, :]).then_inc(h2_in[t], 16)

            def store_out(b, t):
                sp.wait_ge(o_done, b * 8 + (4 + t) + 3)
                sp.dma_start(out[bass.ds(b * BT + t * P, P), :], total[:, t, :]).then_inc(out_dma[t], 16)

            sp.dma_start(ident[:], ident_d).then_inc(const_in, 16)
            for i, g in enumerate((g_out, g_mlp_pre, g_ple)):
                sp.dma_start(gate_in[:, i, :], g).then_inc(const_in, 16)
            for i, g in enumerate(gains):
                sp.dma_start(g_row[:, i, :], row_broadcast(g)).then_inc(const_in, 16)
            load_y(None, 0, 0)
            for C in range(NR4):
                sp.dma_start(w_raw[:, C, :], w_tail[NFF + C]).then_inc(w_dma[C], 16)
            for t in range(TT):
                sp.dma_start(res[:, t, :], x[t * P:(t + 1) * P, :]).then_inc(x_dma[t], 16)
            for t in range(1, TT):
                load_y(None, 0, t)
            for C in range(NR4, NG1 + NR4):
                load_w(C, (NFF + C) if C < NG1 else C - NG1, C % NR4)

            def body(b, u):
                row = ((b + 1) % NBLK) * BT
                for i in range(NR4, NCHB + NR4):
                    load_w(b * NCHB + (NG1 + i), i % NCHB, (u * NCHB + i) % NR4)
                    if i in LOAD_Y:
                        load_y(b, row, LOAD_Y[i])
                    if i == P_AT - 8:
                        sp.wait_ge(xn_done, turn_at(b) + 4)
                        sp.sem_inc(sp_step, 1)
                        sp.dma_start(y_in[:].rearrange("p (c n) -> p c n", c=2),
                                     pT_d[:, bass.ds(b * BT, BT)].rearrange("(c p) n -> p c n", p=P)
                                     ).then_inc(y_dma, 16)
                    t = i - (NFF + 7)
                    if 0 <= t < TT:
                        sp.wait_ge(h_done, h_at(b) + t + 1)
                        sp.dma_start(scr["h2"][t * P:(t + 1) * P, :], res[:, t, :]).then_inc(h2_out[t], 16)
                    if 1 <= t <= TT:
                        sp.wait_ge(xn_done, turn_at(b) + 4 + t)
                        sp.wait_ge(h2_out[t - 1], b * 16 + 16)
                        sp.sem_inc(sp_step, 1)
                        sp.dma_start(res[:, t - 1, :], x[bass.ds(row + (t - 1) * P, P), :]).then_inc(x_dma[t - 1], 16)
                    if i in (NCHB - 3, NCHB - 2):
                        for t in (2 * (i - NCHB + 3), 2 * (i - NCHB + 3) + 1):
                            load_h2(b, t)
                for t in range(TT):
                    store_out(b, t)

            blocks(sp, body)
            for s in out_dma:
                sp.wait_ge(s, 16 * (NBLK + 1))
            for s in w_dma:
                sp.wait_ge(s, 16 * (NG1 + NBLK * NCHB + NR4) // NR4)

        @block.gpsimd
        def _(pool):
            pool.sem_inc(f_mul, 2)
            pool.sem_inc(o_done, 2)
            pool.sem_inc(p_lo, 1)
            for s in out_dma:
                pool.sem_inc(s, 16)

            def split(C, slot, half, nth):
                pool.wait_ge(w_dma[slot], nth * 16)
                if not (isinstance(C, int) and C < NSPL):
                    pool.wait_ge(w_used, C)
                pool.sem_inc(pool_step, 1)
                pool.tensor_scalar(w_sp[0][:, half, :], w_raw[:, slot, :], 1.0, 0.0, ALU.mult, ALU.add).then_inc(w_hi, 1)
                pool.wait_ge(w_hi, C + 1)
                pool.tensor_tensor(w_sp[1][:, half, :], w_raw[:, slot, :], w_sp[0][:, half, :].bitcast(F32),
                                   ALU.subtract).then_inc(w_lo, 1)

            for C in range(NG1):
                split(C, C % NR4, C % NSPL, C // NR4 + 1)
            with pool.Fori(0, NBLK // 2) as it:
                for i in range(2 * NCHB):
                    split(it * (2 * NCHB) + (NG1 + i), i % NR4, i % NSPL,
                          it * (2 * NCHB // NR4) + (NG1 // NR4 + i // NR4 + 1))

        @block.tensor
        def _(pe):
            def turn(i, t):
                pe.wait_ge(xn_done, i + 1)
                for half in range(2):
                    if not (isinstance(i, int) and i == 0):
                        pe.wait_ge(lo_done, i * 2 + half - 1)
                    for j in range(4):
                        kk = 4 * half + j
                        mm = pe.transpose(tp[half][:, j * P:(j + 1) * P], xn[:, t % 2, kk * P:(kk + 1) * P], ident[:])
                    mm.then_inc(tp_done, 1)

            def chunk(C, half, kind, b, what, xs):
                pe.wait_ge(w_lo, C + 1)
                first_of_chunk = [True]

                def product(dst, lhs, rhs, start, stop):
                    mm = pe.matmul(dst, lhs, rhs, start=start, stop=stop)
                    if first_of_chunk[0]:
                        mm.then_inc(w_used, 1)
                        first_of_chunk[0] = False
                    return mm

                if kind == "f":
                    g, j = what[0], what[1]
                    if g == 0 and j < 2:
                        pe.wait_ge(o_done, b * 8 + 2)
                    else:
                        pe.wait_ge(f_relu, f_at(b) + (NF * g + j - 1))
                    w = [a[:, half, :].rearrange("p (k n) -> p k n", k=KD) for a in w_sp]
                    for kk in range(KD):
                        for q, (a, m) in enumerate(PAIRS):
                            mm = product(fb[j % 2][:], w[a][:, kk, :], xs[m][:, kk, :],
                                         kk == 0 and q == 0, kk == KD - 1 and q == 2)
                    mm.then_inc(f_done, 1)
                    return
                g, n, pair = what
                w = [a[:, half, :].rearrange("p (k n) -> p k n", k=2) for a in w_sp]
                src = {"g2": fT, "ple": pT}.get(kind, xs)
                if kind == "g2" and n == 0:
                    pe.wait_ge(f_lo, f_at(b) + (NF * g + 2 * pair + 2))
                first, last = pair == 0, pair == 3 or kind == "ple"
                for t in range(TT):
                    dst = fb[t % 2][:] if kind == "ple" else acc[t][:]
                    if kind == "ple":
                        if not (n == 0 and t < 2):
                            pe.wait_ge(prod_done, b * 8 + (4 * n + t - 1))
                    elif first:
                        if kind == "g2" and g == 0:
                            pe.wait_ge(ev_act, act_at(b) + (4 * n - 4 + t + 1))
                        elif kind == "g2" and g == 1 and n == 0:
                            pe.wait_ge(ev_act, act_at(b) + (4 + t + 1))
                        elif kind == "g2":
                            pe.wait_ge(ev_dve, dve_at(b) + (8 * (g - 1) + 4 * n - 4 + t + 1))
                        elif kind == "g1" and n == 0:
                            if b is not None:
                                pe.wait_ge(ev_dve, dve_at(b) + (20 + t + 1))
                        elif kind == "g1":
                            pe.wait_ge(ev_act, t + 1 if b is None else act_at(b) + (8 + t + 1))
                        else:
                            pe.wait_ge(ev_act, act_at(b) + (12 + 4 * n + t + 1))
                    for kk in range(2):
                        for q, (a, m) in enumerate(PAIRS):
                            mm = product(dst, src[a][:, 2 * pair + kk, t * P:(t + 1) * P], w[m][:, kk, :],
                                         first and kk == 0 and q == 0, last and kk == 1 and q == 2)
                    if last:
                        mm.then_inc(ple_done if kind == "ple" else acc_done, 1)

            pe.wait_ge(const_in, 96)
            for t in range(TT):
                turn(t, t)
            pe.wait_ge(lo_done, 2 * TT)
            for C, c in enumerate(G1):
                chunk(C, C % NSPL, c[0], None, c[1:], xT[1])
            for t in range(TT):
                turn(TT + t, t)

            def body(b, u):
                C = b * NCHB + NG1
                pe.wait_ge(lo_done, turn_at(b) * 2)
                for i, c in enumerate(FF):
                    chunk(C + i, i % NSPL, c[0], b, c[1:], xT[u])
                    if i in TURN_Y:
                        turn(turn_at(b) + TURN_Y[i], TURN_Y[i])
                pe.wait_ge(lo_done, turn_at(b) * 2 + 8)
                for i, c in enumerate(G1):
                    chunk(C + (NFF + i), (NFF + i) % NSPL, c[0], b, c[1:], xT[1 - u])
                    if i in TURN_Z:
                        turn(turn_at(b) + (4 + TURN_Z[i]), TURN_Z[i])
                pe.wait_ge(lo_done, turn_at(b) * 2 + 16)
                pe.wait_ge(p_lo, b + 2)
                for i, c in enumerate(G3):
                    at = NFF + NG1 + i
                    chunk(C + at, at % NSPL, c[0], b, c[1:], xT[u])
                    if i in TURN_X:
                        turn(turn_at(b) + (8 + TURN_X[i]), TURN_X[i])

            blocks(pe, body)

        @block.scalar
        def _(act):
            def root(i, slot, parts):
                act.wait_ge(rec_done, i + 1)
                act.activation(rstd[:, slot, 0:parts], rec[:, slot, 0:parts], ACT.Sqrt).then_inc(rt_done, 1)

            def norms(at, h0, sums_read):
                def square(n):
                    place, t = SQUARES[n]
                    if place == 1:
                        act.wait_ge(*sums_read(t))
                    else:
                        act.wait_ge(h_done, h0 + (t + 1))
                    act.activation(junk[:, n % 2, :], (total if place == 1 else res)[:, t, :], ACT.Square,
                                   accum_out=ssq[:, TT + n, 0:1]).then_inc(sq_done, 1)

                for what, n in (("s", 0), ("s", 1), ("r", 0), ("r", 1), ("s", 2), ("s", 3), ("r", 2), ("s", 4), ("r", 3),
                                ("s", 5), ("r", 4), ("r", 5), ("s", 6), ("s", 7), ("r", 6), ("r", 7)):
                    if what == "s":
                        square(n)
                    else:
                        root(at + n, TT + n, 1)

            def y_norm(i, t, count):
                act.wait_ge(y_dma, count)
                for part in range(2):
                    at = slice(part * D_AB, (part + 1) * D_AB)
                    ins = act.activation(junk[:, 0, at], y_in[:, at], ACT.Square, accum_out=ssq[:, t % 4, part:part + 1])
                ins.then_inc(sq_done, 1)
                root(i, t % 4, 2)

            def turned_hi(i, t, gain, dst):
                for half in range(2):
                    act.wait_ge(tp_done, i * 2 + half + 1)
                    for j in range(4):
                        kk = 4 * half + j
                        ins = act.activation(dst[0][:, kk, t * P:(t + 1) * P], tp[half][:, j * P:(j + 1) * P], ACT.Copy,
                                             scale=gate_in[:, gain, kk:kk + 1])
                    ins.then_inc(hi_done, 1)

            def to_total(count, n, t):
                act.wait_ge(acc_done, count)
                act.activation(total[:, t, n * BANK:(n + 1) * BANK], acc[t][:], ACT.Copy).then_inc(ev_act, 1)

            act.wait_ge(const_in, 96)
            for t in range(TT):
                y_norm(t, t, 32 * (t + 1))
                turned_hi(t, t, 0, xT[1])
            for n in range(2):
                for t in range(TT):
                    to_total(4 * n + t + 1, n, t)
            norms(4, 0, lambda t: (ev_act, 4 + t + 1))
            for t in range(TT):
                turned_hi(TT + t, t, 1, xT[0])

            def body(b, u):
                def hidden(g, j):
                    F = f_at(b) + (NF * g + j)
                    act.wait_ge(f_done, F + 1)
                    if g == 0 and j < 2:
                        act.wait_ge(o_done, b * 8 + 2)
                    act.wait_ge(f_mul, F + 1)
                    act.activation(rl[:, j % 2, :], fb[j % 2][:], ACT.Relu).then_inc(f_relu, 1)
                    act.wait_ge(f_relu, F + 1)
                    act.activation(fT[0][:, j, :], rl[:, j % 2, :], ACT.Square).then_inc(f_hi, 1)

                for i, c in enumerate(FF):
                    if c[0] == "f":
                        hidden(c[1], c[2])
                    elif c[1] == 0 and c[3] == 3:
                        for t in range(TT):
                            if c[2] == 0:
                                act.wait_ge(out_dma[t], b * 16 + 16)
                            to_total(acc_at(b) + (4 * c[2] + t + 1), c[2], t)
                    if i in NORM_Y:
                        t = NORM_Y[i]
                        y_norm(norm_at(b) + t, t, b * 144 + (32 * TT + 32 * (t + 1)))
                    if i in TURN_Y:
                        t = TURN_Y[i]
                        turned_hi(turn_at(b) + t, t, 0, xT[1 - u])
                    if i == P_AT:
                        act.wait_ge(y_dma, b * 144 + (32 * 4 * 2 + 16))
                        act.activation(pT[0][:].rearrange("p c n -> p (c n)"), y_in[:], ACT.Copy).then_inc(p_hi, 1)

                z_hi = lambda t: turned_hi(turn_at(b) + (4 + t), t, 2, xT[u])
                x_hi = lambda t: turned_hi(turn_at(b) + (8 + t), t, 1, xT[1 - u])
                norms(norm_at(b) + 4, h_at(b), lambda t: (ev_dve, dve_at(b) + (20 + t + 1)))
                z_hi(0)
                for t in range(TT):
                    to_total(acc_at(b) + (32 + t + 1), 0, t)
                z_hi(1)
                z_hi(2)
                z_hi(3)
                for t in range(TT):
                    to_total(acc_at(b) + (36 + t + 1), 1, t)

                def gates(n):
                    for t in range(TT):
                        q = 4 * n + t
                        act.wait_ge(acc_done, acc_at(b) + (40 + q + 1))
                        if q < 2:
                            act.wait_ge(f_mul, f_at(b) + (4 * NF + 2))
                        else:
                            act.wait_ge(prod_done, b * 8 + (q - 1))
                        act.activation(rl[:, t % 2, :], acc[t][:], ACT.Sigmoid).then_inc(ev_act, 1)

                norms(norm_at(b) + 12, h_at(b) + 4, lambda t: (ev_act, act_at(b) + (12 + t + 1)))
                x_hi(0)
                x_hi(1)
                gates(0)
                x_hi(2)
                x_hi(3)
                gates(1)

            blocks(act, body)

        @block.vector
        def _(ve):
            def inverse(i, slot, parts, width):
                ve.wait_ge(sq_done, i + 1)
                ve.tensor_scalar(ms[:, slot, 0:parts], ssq[:, slot, 0:parts], 1.0 / width, EPS, ALU.mult, ALU.add
                                 ).then_inc(var_done, 1)
                ve.wait_ge(var_done, i + 1)
                ve.reciprocal(rec[:, slot, 0:parts], ms[:, slot, 0:parts]).then_inc(rec_done, 1)

            def normed(i, slot, T, t, src, parts=1):
                ve.wait_ge(rt_done, i + 1)
                if not (isinstance(T, int) and T < 2):
                    ve.wait_ge(tp_done, T * 2 - 2)
                for part in range(parts):
                    at = slice(part * (D // parts), (part + 1) * (D // parts))
                    ins = ve.tensor_scalar(xn[:, t % 2, at], src[:, at], rstd[:, slot, part:part + 1], None, ALU.mult)
                ins.then_inc(xn_done, 1)

            def turned_lo(i, t, gain, dst):
                for half in range(2):
                    ve.wait_ge(hi_done, i * 2 + half + 1)
                    for j in range(4):
                        kk = 4 * half + j
                        at = (slice(None), kk, slice(t * P, (t + 1) * P))
                        ins = ve.scalar_tensor_tensor(out=dst[1][at], in0=tp[half][:, j * P:(j + 1) * P],
                                                      scalar=gate_in[:, gain, kk:kk + 1], in1=dst[0][at].bitcast(F32),
                                                      op0=ALU.mult, op1=ALU.subtract)
                    ins.then_inc(lo_done, 1)

            def residuals(at, h0, which, T, x_read, lo):
                def inv(n):
                    inverse(at + n, TT + n, 1, D)

                def added(t):
                    n = SQUARES.index((1, t))
                    ve.wait_ge(rt_done, at + n + 1)
                    if x_read is not None:
                        ve.wait_ge(x_dma[t], x_read)
                    ve.scalar_tensor_tensor(out=total[:, t, :], in0=total[:, t, :], scalar=rstd[:, TT + n, 0:1],
                                            in1=g_row[:, which, :], op0=ALU.mult, op1=ALU.mult).then_inc(gained, 1)
                    ve.wait_ge(gained, h0 + (t + 1))
                    ve.tensor_tensor(res[:, t, :], res[:, t, :], total[:, t, :], ALU.add).then_inc(h_done, 1)

                def unit(t):
                    n = SQUARES.index((2, t))
                    normed(at + n, TT + n, T + t, t, res[:, t, :])

                for what, n in ((inv, 0), (inv, 1), (added, 0), (inv, 2), (added, 1), (inv, 3), (added, 2), (inv, 4),
                                (inv, 5), (added, 3), (unit, 0), (unit, 1), (inv, 6), (inv, 7), (lo, 0), (unit, 2),
                                (lo, 1), (unit, 3)):
                    what(n)

            ve.wait_ge(const_in, 96)
            for t in range(TT):
                inverse(t, t, 2, D_AB)
                normed(t, t, t, t, y_in[:], 2)
                turned_lo(t, t, 0, xT[1])
            first_lo = lambda t: turned_lo(TT + t, t, 1, xT[0])
            residuals(4, 0, 0, TT, 16, first_lo)
            first_lo(2)
            first_lo(3)

            def body(b, u):
                def hidden(g, j):
                    F = f_at(b) + (NF * g + j)
                    ve.wait_ge(f_relu, F + 1)
                    ve.tensor_tensor(fs[:, j % 2, :], rl[:, j % 2, :], rl[:, j % 2, :], ALU.mult).then_inc(f_mul, 1)
                    ve.wait_ge(f_mul, F + 3)
                    ve.wait_ge(f_hi, F + 1)
                    ve.tensor_tensor(fT[1][:, j, :], fs[:, j % 2, :], fT[0][:, j, :].bitcast(F32), ALU.subtract
                                     ).then_inc(f_lo, 1)

                for i, c in enumerate(FF):
                    if c[0] == "f":
                        hidden(c[1], c[2])
                    elif c[1] > 0 and c[3] == 3:
                        for t in range(TT):
                            q = 4 * c[2] + t
                            ve.wait_ge(acc_done, acc_at(b) + (8 * c[1] + q + 1))
                            if c[1] == 1:
                                ve.wait_ge(ev_act, act_at(b) + (q + 1))
                            else:
                                ve.wait_ge(ev_dve, dve_at(b) + (8 * (c[1] - 2) + q + 1))
                            at = total[:, t, c[2] * BANK:(c[2] + 1) * BANK]
                            ve.tensor_tensor(at, acc[t][:], at, ALU.add).then_inc(ev_dve, 1)
                    if i in NORM_Y:
                        t = NORM_Y[i]
                        inverse(norm_at(b) + t, t, 2, D_AB)
                        normed(norm_at(b) + t, t, turn_at(b) + t, t, y_in[:], 2)
                    if i in TURN_Y:
                        t = TURN_Y[i]
                        turned_lo(turn_at(b) + t, t, 0, xT[1 - u])
                    if i == P_AT:
                        ve.wait_ge(p_hi, b + 1)
                        ve.tensor_tensor(pT[1][:].rearrange("p c n -> p (c n)"), y_in[:],
                                         pT[0][:].rearrange("p c n -> p (c n)").bitcast(F32), ALU.subtract
                                         ).then_inc(p_lo, 1)

                z_lo = lambda t: turned_lo(turn_at(b) + (4 + t), t, 2, xT[u])
                x_lo = lambda t: turned_lo(turn_at(b) + (8 + t), t, 1, xT[1 - u])
                residuals(norm_at(b) + 4, h_at(b), 1, turn_at(b) + 4, None, z_lo)
                z_lo(2)
                z_lo(3)

                def outputs(n):
                    for t in range(TT):
                        q = 4 * n + t
                        ve.wait_ge(ev_act, act_at(b) + (16 + q + 1))
                        ve.wait_ge(ple_done, b * 8 + (q + 1))
                        ve.tensor_tensor(fs[:, t % 2, :], fb[t % 2][:], rl[:, t % 2, :], ALU.mult).then_inc(prod_done, 1)
                        ve.wait_ge(prod_done, b * 8 + (q + 1))
                        if n == 0:
                            ve.wait_ge(h2_in[t], b * 16 + 16)
                        at = total[:, t, n * BANK:(n + 1) * BANK]
                        ve.tensor_tensor(at, fs[:, t % 2, :], at, ALU.add).then_inc(o_done, 1)

                residuals(norm_at(b) + 12, h_at(b) + 4, 0, turn_at(b) + 8, b * 16 + 32, x_lo)
                outputs(0)
                x_lo(2)
                x_lo(3)
                outputs(1)

            blocks(ve, body)


def chunked(w, half_k, width):
    kk, n = w.shape[0] // P, w.shape[1] // width
    a = w.reshape(kk // half_k, half_k, P, n, width).transpose(3, 0, 2, 1, 4)
    return a.reshape(-1, P, half_k * width)


def token_order():
    return np.arange(S).reshape(SUB, RES).T.reshape(-1)


def rope_constants():
    grid = 64
    tok = token_order()
    n_axis = HD // 4
    inv = np.float32(10000.0) ** (-np.arange(n_axis, dtype=np.float32) / np.float32(n_axis))
    row, col = (tok // grid).astype(np.float32), (tok % grid).astype(np.float32)
    ang = np.concatenate([row[:, None] * inv, col[:, None] * inv], -1).astype(np.float32)
    cos, sin = np.cos(ang), np.sin(ang)
    return np.concatenate([cos, cos, -sin, sin], -1).astype(np.float32)


def bias_constants():
    m = np.arange(2 * BANK) - (BANK - 1)
    onehot = np.zeros((32, 8, 2 * BANK), np.float32)
    log_count = np.full((8, 2 * BANK), NEG, np.float32)
    for v, diff in enumerate((-3, -2, -1, None, 1, 2, 3, 0)):
        if diff is None:
            continue
        rel = RES * m + diff
        dist = np.abs(rel)
        count = (dist <= 64) * 1 + ((dist <= 256) & (rel % 4 == 0)) + ((dist <= 1024) & (rel % 16 == 0))
        large = 8 + (np.log(np.maximum(dist, 8).astype(np.float32) / np.float32(8)) / np.float32(math.log(128.0))
                     * np.float32(8)).astype(np.int32)
        bucket = np.where(rel > 0, 16, 0) + np.where(dist < 8, dist, np.minimum(large, 15))
        held = count > 0
        log_count[v, held] = np.log(count[held].astype(np.float64))
        onehot[bucket[held], v, np.flatnonzero(held)] = 1.0
    return np.concatenate([onehot.reshape(32, -1), log_count.reshape(1, -1)], 0)


def lay_out(x, p, w_in, g_attn_pre, g_q, g_k, g_out_a, g_out_b, w_out, g_attn_post, rel_bias,
            g_mlp_pre, w_ff1, w_ff2, g_mlp_post, g_ple, w_ple_gate, w_ple_proj):
    order = token_order()
    xo = x[0][order]
    w = w_in[0]
    by_tile = lambda g: g.reshape(KD, P).T
    ff = [a for g in range(0, D_FF, D) for a in (chunked(w_ff1[0][:, g:g + D], KD, P),
                                                  chunked(w_ff2[0][g:g + D], 2, BANK))]
    gate, ple = chunked(w_ple_gate[0], 2, BANK), chunked(w_ple_proj[0], 2, BANK)
    return {
        "rel_bias": np.concatenate([rel_bias, np.ones((1, NHB), np.float32)], 0),
        "onehot": bias_constants(),
        "x": np.concatenate([xo, xo[:BT]], 0),
        "w_in": np.concatenate([chunked(w[:, 0:512], 4, 512), chunked(w[:, 512:768], 8, 256),
                                chunked(w[:, 768:], 4, 512)], 0),
        "rope": rope_constants(),
        "ident": np.eye(P, dtype=np.float32),
        "fold": np.concatenate([np.eye(HD, dtype=np.float32)] * 2, 0),
        "w_tail": np.concatenate(ff + [chunked(w_out[0], 2, BANK), gate[:4], ple[:1], gate[4:], ple[1:]], 0),
        "g_out": by_tile(np.concatenate([g_out_a[0], g_out_b[0]])),
        "g_mlp_pre": by_tile(g_mlp_pre[0]),
        "g_ple": by_tile(g_ple[0]),
        "g_attn_pre": g_attn_pre[0], "g_q": g_q[0], "g_k": g_k[0],
        "g_attn_post": g_attn_post[0], "g_mlp_post": g_mlp_post[0],
        "pT": p[0, 0][order].T,
    }


def layer(nc, rel_bias, onehot, x, w_in, rope, ident, fold, w_tail, g_out, g_mlp_pre, g_ple,
          g_attn_pre, g_q, g_k, g_attn_post, g_mlp_post, pT, out):
    shapes = {"qA": (S, NHA * 2 * HD), "kA": (S, NKV * 2 * HD), "vA": (S, NKV * HD), "qB": (S, 2 * D_AB), "kB": (S, 2 * D_AB),
              "vB": (S + 2 * PAD, D_AB), "bias": (8, 8 * 2 * BANK), "table": (NHB, P, ROWS_W),
              "yA": (S + P, D_AB), "yB": (S, D_AB), "h2": (BT, D)}
    scr = {n: nc.dram_tensor(f"scr_{n}", shape, F32, kind="Internal").ap() for n, shape in shapes.items()}
    project_phase(nc, x, w_in, g_attn_pre, g_q, g_k, rope, ident, rel_bias, onehot, scr)
    mixer_a_phase(nc, ident, fold, scr)
    mixer_b_phase(nc, ident, fold, scr)
    feed_phase(nc, x, w_tail, (g_attn_post, g_mlp_post), g_out, g_mlp_pre, g_ple, pT, ident, scr, out)


def kernel(**inputs):
    import numpy as _np
    import concourse.bacc as _bacc
    from concourse import mybir as _mybir
    from concourse.bass_utils import run_bass_kernel_spmd as _run

    nc = _bacc.Bacc("TRN2", target_bir_lowering=False, num_devices=1)
    arrays = {f"{n}_dram": _np.ascontiguousarray(a) for n, a in
              lay_out(**{n: _np.asarray(a) for n, a in inputs.items()}).items()}
    args = [nc.dram_tensor(n, a.shape, _mybir.dt.from_np(a.dtype), kind="ExternalInput").ap() for n, a in arrays.items()]
    out = nc.dram_tensor("out_dram", (S, D), _mybir.dt.float32, kind="ExternalOutput").ap()
    layer(nc, *args, out)
    got = _run(nc, [arrays], core_ids=[0]).results[0]["out_dram"]
    y = _np.empty_like(got)
    y[token_order()] = got
    return y[None]
```

```python
import math
from contextlib import ExitStack

import numpy as np

import concourse.bass as bass
from concourse import mybir
from concourse.alu_op_type import AluOpType as ALU

F32 = mybir.dt.float32
F32R = mybir.dt.float32r
ACT = mybir.ActivationFunctionType
AXX = mybir.AxisListType.X

P = 128
D = 1024
S = 2048
HD = 64
NHA, NKV, NHB = 8, 2, 8
D_AB = 512
D_FF = 4096
KD = D // P
BT = 512
TT = BT // P
NBLK = S // BT
RES = 4
SUB = S // RES
PAD = 16
EPS = 1e-6
NEG = -1e30
BANK = 512
CH = 2048
NBIAS = 33
NRAW, NSPL = 3, 2
OWN_W = 7 * P
TABLE_W = OWN_W + 7 * (P + 2 * PAD)
ROWS_W = TABLE_W + 8 * P
PAIRS = ((0, 0), (0, 1), (1, 0))


class Kit:

    def __init__(self, nc, ctx, phase):
        self.nc, self.ctx, self.phase = nc, ctx, phase

    def sb(self, name, shape, dt=F32):
        return self.ctx.enter_context(self.nc.sbuf_tensor(f"{self.phase}_{name}", shape, dt))

    def banks(self, n=8):
        return [self.ctx.enter_context(self.nc.psum_tensor(f"{self.phase}_bank{i}", [P, BANK], F32)) for i in range(n)]

    def sem(self, name):
        return self.ctx.enter_context(self.nc.semaphore(f"{self.phase}_{name}"))

    def sems(self, name, n):
        return [self.sem(f"{name}{i}") for i in range(n)]


def row_broadcast(row):
    n = row.shape[-1]
    return bass.AP(row.tensor, row.offset, [[0, P], [1, n]])


def project_phase(nc, x, w_in, g_pre, g_q, g_k, rope, ident_d, rel_bias, onehot, scr, step):
    STEPS_1, STEPS = 4, 10
    NCH = 9
    NG = 5
    GROUP_OF = [0, 0, 1, 2, 2, 3, 3, 4, 4]
    BIAS_W = ROWS_W // (2 * NBLK)
    BIAS_AT = {0: 0, 4: 1}
    NORM_AT = {0: (0, 1), 3: (2,), 5: (3,)}
    with ExitStack() as ctx:
        k = Kit(nc, ctx, "proj")
        ident = k.sb("ident", [P, P])
        g_row = k.sb("g_row", [P, D])
        gq_row = k.sb("gq_row", [P, HD])
        gk_row = k.sb("gk_row", [P, HD])
        rb = k.sb("rb", [NBIAS, NHB])
        oh = k.sb("oh", [NBIAS, 2, BIAS_W])
        vec = k.sb("vec", [NHB, 2, BIAS_W])
        x_t = k.sb("x_t", [P, TT, D])
        junk = k.sb("junk", [P, 2, D], mybir.dt.bfloat16)
        ssq = k.sb("ssq", [P, 2])
        ms = k.sb("ms", [P, 2])
        rec = k.sb("rec", [P, 2])
        rstd = k.sb("rstd", [P, 2])
        xn = k.sb("xn", [P, 2, D])
        xT = [[k.sb(f"xT{u}{h}", [P, KD, BT], F32R) for h in range(2)] for u in range(2)]
        w_raw = k.sb("w_raw", [P, NRAW, CH])
        w_sp = [k.sb(f"w_split{h}", [P, NSPL, CH], F32R) for h in range(2)]
        rope_t = k.sb("rope_t", [P, 2, TT, 2 * HD])
        qs = k.sb("qs", [P, TT, D_AB])
        ks = k.sb("ks", [P, TT, NKV * HD])
        st = k.sb("st", [P, TT, BANK])
        t1 = k.sb("t1", [P, D_AB])
        t2 = k.sb("t2", [P, D_AB])
        hs = k.sb("hs", [P, TT, 4, 8])
        qo = k.sb("qo", [P, 2, NHA * 2 * HD])
        ko = k.sb("ko", [P, 2, NKV * 2 * HD])
        zrow = k.sb("zrow", [PAD, D_AB])
        bank = k.banks()
        acc, tp, bias_bank = bank[0:4], bank[4:6], bank[6:8]

        first_in, const_in = k.sem("first_in"), k.sem("const_in")
        oh_dma, bias_mm, vec_done = k.sems("oh_dma", 2), k.sem("bias_mm"), k.sem("vec_done")
        bias_out = k.sems("bias_out", 2)
        x_in = k.sems("x_in", TT)
        rope_in = k.sem("rope_in")
        ssq_done, rec_done, rstd_done, xn_done = (k.sem(n) for n in ("ssq_done", "rec_done", "rstd_done", "xn_done"))
        tp_done, hi_done, lo_done = (k.sem(n) for n in ("tp_done", "hi_done", "lo_done"))
        w_in_dma = k.sems("w_dma", NRAW)
        w_hi, w_lo, w_used = k.sem("w_hi"), k.sem("w_lo"), k.sem("w_used")
        acc_done, evicted = k.sem("acc_done"), k.sem("evicted")
        qs_free = k.sem("qs_free")
        ks_free = k.sem("ks_free")
        qo_ready, ko_ready = k.sem("qo_ready"), k.sem("ko_ready")
        st_out = k.sems("st_out", TT)
        qo_out, ko_out = k.sems("qo_out", 2), k.sems("ko_out", 2)
        pad_out = k.sem("pad_out")
        dve = k.sem("dve")
        head_rstd, var_step = k.sem("head_rstd"), k.sem("var_step")
        block = ctx.enter_context(nc.Block())

        @block.sync
        def _(sp):
            for t in range(TT):
                sp.dma_start(x_t[:, t, :], x[t * P:(t + 1) * P, :]).then_inc(x_in[t], 16)
                if t == 0:
                    sp.dma_start(ident[:], ident_d).then_inc(first_in, 16)
                    sp.dma_start(g_row[:], row_broadcast(g_pre)).then_inc(first_in, 16)
            sp.dma_start(gq_row[:], row_broadcast(g_q)).then_inc(const_in, 16)
            sp.dma_start(gk_row[:], row_broadcast(g_k)).then_inc(const_in, 16)
            sp.dma_start(rb[:], rel_bias).then_inc(const_in, 16)
            sp.wait_ge(pad_out, 1)
            for row in (0, PAD + S):
                sp.dma_start(scr["vB"][row:row + PAD, :], zrow[:]).then_inc(pad_out, 16)
            with sp.Fori(0, NBLK // 2) as it:
                for u in range(2):
                    b = it * 2 + u
                    sp.dma_start(rope_t[:, u, :, :], rope[bass.ds(b * BT, BT), :].rearrange("(t p) c -> p t c", p=P)
                                 ).then_inc(rope_in, 16)
                    for i in range(NCH):
                        c = NCH * u + i
                        sp.wait_ge(w_lo, it * (2 * NCH) + c + 1)
                        sp.dma_start(w_raw[:, c % NRAW, :], w_in[i]).then_inc(w_in_dma[c % NRAW], 16)
                        if i % 2 == 0 and i // 2 < TT:
                            t = i // 2
                            sp.wait_ge(xn_done, b * TT + t + 1)
                            sp.dma_start(x_t[:, t, :], x[bass.ds((b + 1) * BT + t * P, P), :]).then_inc(x_in[t], 16)
                        if i in BIAS_AT:
                            j = BIAS_AT[i]
                            sp.wait_ge(bias_mm, b * 2 + j + 1)
                            sp.sem_inc(step, 1)
                            sp.dma_start(oh[:, j, :], onehot[:, bass.ds((b * 2 + j) * BIAS_W, BIAS_W)]
                                         ).then_inc(oh_dma[j], 16)
                        if i == 5:
                            for t in range(TT):
                                sp.wait_ge(qo_ready, b * TT + t + 1)
                                sp.dma_start(scr["qA"][bass.ds(b * BT + t * P, P), :], qo[:, t % 2, :]
                                             ).then_inc(qo_out[t % 2], 16)
                        if i == 6:
                            for t in range(TT):
                                sp.wait_ge(ko_ready, b * TT + t + 1)
                                sp.dma_start(scr["kA"][bass.ds(b * BT + t * P, P), :], ko[:, t % 2, :]
                                             ).then_inc(ko_out[t % 2], 16)
            for s in (*qo_out, *ko_out):
                sp.wait_ge(s, 16 * (2 * NBLK + 1))
            for s in st_out:
                sp.wait_ge(s, 16 * (6 * NBLK + 1))
            for s in bias_out:
                sp.wait_ge(s, 16 * (NBLK + 1))
            sp.wait_ge(pad_out, 33)

        @block.gpsimd
        def _(pool):
            pool.memset(zrow[:], 0.0).then_inc(pad_out, 1)
            pool.sem_inc(w_lo, NRAW)
            pool.sem_inc(w_used, 1)
            pool.sem_inc(evicted, TT)
            pool.sem_inc(qs_free, TT)
            pool.sem_inc(ks_free, TT)
            pool.sem_inc(bias_mm, 2)
            pool.sem_inc(vec_done, 2)
            for s in (*bias_out, *st_out, *qo_out, *ko_out):
                pool.sem_inc(s, 16)
            with pool.Fori(0, NBLK // 2) as it:
                for c in range(2 * NCH):
                    slot, half = c % NRAW, c % NSPL
                    pool.wait_ge(w_in_dma[slot], it * (16 * 2 * NCH // NRAW) + 16 * (c // NRAW + 1))
                    prev, pu = (c - NSPL) % NCH, (c - NSPL) // NCH
                    if prev == NCH - 1 or GROUP_OF[prev + 1] != GROUP_OF[prev]:
                        pool.wait_ge(evicted, it * (2 * NG * TT) + NG * TT * pu + TT + TT * GROUP_OF[prev] + TT)
                    else:
                        pool.wait_ge(w_used, it * 8 + 4 * pu + [0, 3, 5, 7].index(prev) + 2)
                    pool.sem_inc(step, 1)
                    pool.tensor_scalar(w_sp[0][:, half, :], w_raw[:, slot, :], 1.0, 0.0, ALU.mult, ALU.add
                                       ).then_inc(w_hi, 1)
                    pool.wait_ge(w_hi, it * (2 * NCH) + c + 1)
                    pool.tensor_tensor(w_sp[1][:, half, :], w_raw[:, slot, :], w_sp[0][:, half, :].bitcast(F32),
                                       ALU.subtract).then_inc(w_lo, 1)

        @block.tensor
        def _(pe):
            def turn(nb, t):
                pe.wait_ge(xn_done, nb * TT + t + 1)
                for half in range(2):
                    if not (isinstance(nb, int) and t == 0):
                        pe.wait_ge(lo_done, (nb * TT + t) * 2 + half - 1)
                    for j in range(4):
                        kk = 4 * half + j
                        mm = pe.transpose(tp[half][:, j * P:(j + 1) * P], xn[:, t % 2, kk * P:(kk + 1) * P], ident[:])
                    mm.then_inc(tp_done, 1)

            pe.wait_ge(first_in, 32)
            for t in range(TT):
                turn(0, t)
            pe.wait_ge(const_in, 48)
            with pe.Fori(0, NBLK // 2) as it:
                for u in range(2):
                    b = it * 2 + u
                    pe.wait_ge(lo_done, b * (2 * TT) + 2 * TT)
                    for i in range(NCH):
                        c = NCH * u + i
                        g = GROUP_OF[i]
                        n_k = 8 if g == 1 else 4
                        width = CH // n_k
                        k0 = 4 if i > 0 and GROUP_OF[i - 1] == g else 0
                        first, last = k0 == 0, k0 + n_k == KD
                        pe.wait_ge(w_lo, it * (2 * NCH) + NRAW + c + 1)
                        w = [h[:, c % NSPL, :].rearrange("p (k n) -> p k n", k=n_k) for h in w_sp]
                        for t in range(TT):
                            if first:
                                pe.wait_ge(evicted, b * (NG * TT) + TT * g + t + 1)
                            for kk in range(n_k):
                                for q, (a, m) in enumerate(PAIRS):
                                    mm = pe.matmul(acc[t][:, 0:width], xT[u][a][:, k0 + kk, t * P:(t + 1) * P],
                                                   w[m][:, kk, :], start=first and kk == 0 and q == 0,
                                                   stop=last and kk == n_k - 1 and q == 2)
                            if last:
                                mm.then_inc(acc_done, 1)
                        if not last:
                            mm.then_inc(w_used, 1)
                        if i % 2 == 1:
                            turn(b + 1, i // 2)
                        if i in BIAS_AT:
                            j = BIAS_AT[i]
                            pe.wait_ge(oh_dma[j], b * 16 + 16)
                            pe.wait_ge(vec_done, b * 2 + j + 1)
                            pe.sem_inc(step, 1)
                            pe.matmul(bias_bank[j][0:NHB, 0:BIAS_W], rb[:], oh[:, j, :], start=True, stop=True
                                      ).then_inc(bias_mm, 1)

        @block.scalar
        def _(act):
            def squares(nb, t):
                act.wait_ge(x_in[t], nb * 16 + 16)
                act.activation(junk[:, t % 2, :], x_t[:, t, :], ACT.Square, accum_out=ssq[:, t % 2:t % 2 + 1]).then_inc(ssq_done, 1)
                act.wait_ge(rec_done, nb * TT + t + 1)
                act.activation(rstd[:, t % 2:t % 2 + 1], rec[:, t % 2:t % 2 + 1], ACT.Sqrt).then_inc(rstd_done, 1)

            def hi_part(nb, t, par):
                for half in range(2):
                    act.wait_ge(tp_done, (nb * TT + t) * 2 + half + 1)
                    act.activation(xT[par][0][:, 4 * half:4 * half + 4, t * P:(t + 1) * P],
                                   tp[half][:].rearrange("p (k n) -> p k n", k=4), ACT.Copy).then_inc(hi_done, 1)

            squares(0, 0)
            for t in range(TT):
                if t < TT - 1:
                    squares(0, t + 1)
                hi_part(0, t, 0)
            with act.Fori(0, NBLK // 2) as it:
                for u in range(2):
                    b = it * 2 + u
                    for i in range(NCH):
                        g = GROUP_OF[i]
                        for t in NORM_AT.get(i, ()):
                            squares(b + 1, t)
                        if i == NCH - 1 or GROUP_OF[i + 1] != g:
                            for t in range(TT):
                                act.wait_ge(acc_done, b * (NG * TT) + TT * g + t + 1)
                                if g == 0:
                                    act.wait_ge(qs_free, b * TT + t + 1)
                                    act.activation(qs[:, t, :], acc[t][:], ACT.Copy).then_inc(evicted, 1)
                                elif g == 1:
                                    act.wait_ge(ks_free, b * TT + t + 1)
                                    act.wait_ge(st_out[t], b * 96 + 16)
                                    act.activation(st[:, t, 0:P], acc[t][:, P:2 * P], ACT.Copy)
                                    act.activation(ks[:, t, :], acc[t][:, 0:P], ACT.Copy).then_inc(evicted, 1)
                                    act.wait_ge(evicted, b * (NG * TT) + TT + TT * g + t + 1)
                                    act.dma_start(scr["vA"][bass.ds(b * BT + t * P, P), :], st[:, t, 0:P]
                                                  ).then_inc(st_out[t], 16)
                                else:
                                    m = g - 1
                                    act.wait_ge(st_out[t], b * 96 + 32 * m)
                                    act.activation(st[:, t, :], acc[t][:], ACT.Copy,
                                                   scale=HD ** -0.5 if g == 2 else 1.0).then_inc(evicted, 1)
                                    act.wait_ge(evicted, b * (NG * TT) + TT + TT * g + t + 1)
                                    if g == 4:
                                        act.dma_start(scr["vB"][bass.ds(b * BT + t * P + PAD, P), :], st[:, t, :]
                                                      ).then_inc(st_out[t], 16)
                                    else:
                                        rows = scr[("qB", "kB")[g - 2]][bass.ds(b * BT + t * P, P), :].rearrange(
                                            "p (h c d) -> p h c d", h=NHB, c=2)
                                        for twice in range(2):
                                            act.dma_start(rows[:, :, twice, :],
                                                          st[:, t, :].rearrange("p (h d) -> p h d", h=NHB)
                                                          ).then_inc(st_out[t], 16)
                            if g <= 1:
                                for t in range(TT):
                                    n = (NHA, NKV)[g]
                                    act.wait_ge(dve, it * (STEPS * 4 * TT) + STEPS * TT * (2 * u + g) + STEPS_1 * (t + 1))
                                    act.activation(hs[:, t, 3, 0:n], hs[:, t, 2, 0:n], ACT.Sqrt,
                                                   scale=(1.0 / HD, 1.0)[g]).then_inc(head_rstd, 1)
                        if i % 2 == 1:
                            hi_part(b + 1, i // 2, 1 - u)
                        if i in BIAS_AT:
                            j = BIAS_AT[i]
                            act.wait_ge(bias_mm, b * 2 + j + 3)
                            act.wait_ge(bias_out[j], b * 16 + 16)
                            act.activation(vec[:, j, :], bias_bank[j][0:NHB, 0:BIAS_W], ACT.Copy).then_inc(vec_done, 1)
                            act.wait_ge(vec_done, b * 2 + j + 3)
                            act.sem_inc(step, 1)
                            act.dma_start(scr["bias"][:, bass.ds((b * 2 + j) * BIAS_W, BIAS_W)], vec[:, j, :]
                                          ).then_inc(bias_out[j], 16)

        @block.vector
        def _(ve):
            def normed(nb, t):
                ve.wait_ge(ssq_done, nb * TT + t + 1)
                a, z = t % 2, t % 2 + 1
                ve.tensor_scalar(ms[:, a:z], ssq[:, a:z], 1.0 / D, EPS, ALU.mult, ALU.add).then_inc(var_step, 1)
                ve.wait_ge(var_step, nb * TT + t + 1)
                ve.reciprocal(rec[:, a:z], ms[:, a:z]).then_inc(rec_done, 1)
                ve.wait_ge(rstd_done, nb * TT + t + 1)
                if not (isinstance(nb, int) and t < 2):
                    ve.wait_ge(tp_done, (nb * TT + t) * 2 - 2)
                ve.scalar_tensor_tensor(out=xn[:, a, :], in0=x_t[:, t, :], scalar=rstd[:, a:z], in1=g_row[:],
                                        op0=ALU.mult, op1=ALU.mult).then_inc(xn_done, 1)

            def lo_part(nb, t, par):
                for half in range(2):
                    at = (slice(None), slice(4 * half, 4 * half + 4), slice(t * P, (t + 1) * P))
                    ve.wait_ge(hi_done, (nb * TT + t) * 2 + half + 1)
                    ve.tensor_tensor(xT[par][1][at], tp[half][:].rearrange("p (k n) -> p k n", k=4),
                                     xT[par][0][at].bitcast(F32), ALU.subtract).then_inc(lo_done, 1)

            def stepper(first):
                done = [0]

                def then(ins, wait=True):
                    done[0] += 1
                    ins.then_inc(dve, 1)
                    if wait:
                        ve.wait_ge(dve, first + done[0])
                return then

            def head_squares(it, u, t, q):
                n, src = (NHA, qs) if q else (NKV, ks)
                g = 0 if q else 1
                b = it * 2 + u
                then = stepper(it * (STEPS * 4 * TT) + (STEPS * TT * (2 * u + g) + STEPS_1 * t))
                x_h, y1 = src[:, t, :].rearrange("p (h d) -> p h d", h=n), t1[:, 0:n * HD].rearrange(
                    "p (h d) -> p h d", h=n)
                ve.wait_ge(evicted, b * (NG * TT) + TT + TT * g + t + 1)
                then(ve.tensor_tensor(y1, x_h, x_h, ALU.mult))
                then(ve.tensor_reduce(hs[:, t, 0, 0:n], y1, AXX, ALU.add))
                then(ve.tensor_scalar(hs[:, t, 1, 0:n], hs[:, t, 0, 0:n], 1.0 / HD, EPS, ALU.mult, ALU.add))
                then(ve.reciprocal(hs[:, t, 2, 0:n], hs[:, t, 1, 0:n]), False)

            def rotated(it, u, t, q):
                n, src, g_h, dst = (NHA, qs, gq_row, qo) if q else (NKV, ks, gk_row, ko)
                g = 0 if q else 1
                b = it * 2 + u
                then = stepper(it * (STEPS * 4 * TT) + (STEPS * TT * (2 * u + g) + STEPS_1 * TT + (STEPS - STEPS_1) * t))
                heads = lambda a: a.rearrange("p (h d) -> p h d", h=n)
                x_h, y1, y2 = heads(src[:, t, :]), heads(t1[:, 0:n * HD]), heads(t2[:, 0:n * HD])
                cos = rope_t[:, u, t:t + 1, 0:HD].broadcast_to([P, n, HD])
                sin = rope_t[:, u, t:t + 1, HD:2 * HD]
                g_all = g_h[:].unsqueeze(1).broadcast_to([P, n, HD])
                ve.wait_ge(head_rstd, b * (2 * TT) + (0 if q else TT) + t + 1)
                then(ve.tensor_tensor(y1, x_h, hs[:, t, 3, 0:n].unsqueeze(2).broadcast_to([P, n, HD]), ALU.mult))
                ve.sem_inc(qs_free if q else ks_free, 1)
                then(ve.tensor_tensor(y2, y1, g_all, ALU.mult))
                if t == 0 and q:
                    ve.wait_ge(rope_in, b * 16 + 16)
                then(ve.tensor_tensor(y1, y2, cos, ALU.mult), False)
                half = HD // 2
                o1 = dst[:, t % 2, :].rearrange("p (h c d) -> p h c d", h=n, c=2)
                ve.wait_ge((qo_out if q else ko_out)[t % 2], b * 32 + 16 * (t // 2 + 1))
                then(ve.tensor_tensor(o1[:, :, 1, 0:half], y2[:, :, half:HD],
                                      sin[:, :, 0:half].broadcast_to([P, n, half]), ALU.mult), False)
                then(ve.tensor_tensor(o1[:, :, 1, half:HD], y2[:, :, 0:half],
                                      sin[:, :, half:HD].broadcast_to([P, n, half]), ALU.mult))
                then(ve.tensor_tensor(o1[:, :, 0, :], y1, o1[:, :, 1, :], ALU.add))
                ve.tensor_copy(o1[:, :, 1, :], o1[:, :, 0, :]).then_inc(qo_ready if q else ko_ready, 1)

            ve.wait_ge(first_in, 32)
            normed(0, 0)
            for t in range(TT):
                if t < TT - 1:
                    normed(0, t + 1)
                lo_part(0, t, 0)
            ve.wait_ge(const_in, 48)
            with ve.Fori(0, NBLK // 2) as it:
                for u in range(2):
                    b = it * 2 + u
                    for i in range(NCH):
                        g = GROUP_OF[i]
                        for t in NORM_AT.get(i, ()):
                            normed(b + 1, t)
                        heads_at = g <= 1 and GROUP_OF[i + 1] != g
                        if heads_at:
                            for t in range(TT):
                                head_squares(it, u, t, g == 0)
                        if i % 2 == 1:
                            lo_part(b + 1, i // 2, 1 - u)
                        if heads_at:
                            for t in range(TT):
                                rotated(it, u, t, g == 0)


def mixer_a_phase(nc, ident_d, fold_d, scr):
    NT = S // P
    G = NHA // NKV
    NC = 2 * G
    NR = 4
    with ExitStack() as ctx:
        k = Kit(nc, ctx, "mixa")
        ident = k.sb("ident", [P, P])
        fold = k.sb("fold", [P, HD])
        k_raw = k.sb("k_raw", [P, NT, NKV * 2 * HD])
        v_raw = k.sb("v_raw", [P, NT, NKV * HD])
        kT = [[k.sb(f"kT{g}{h}", [P, S], F32R) for h in range(2)] for g in range(NKV)]
        v_hl = k.sb("v_hl", [P, NT, NKV, 2 * HD], F32R)
        q_in = k.sb("q_in", [P, NHA * 2 * HD])
        qT = [k.sb(f"qT{g}", [P, G, P], F32R) for g in range(NKV)]
        prob = [k.sb(f"prob{u}", [P, G, S]) for u in range(2)]
        pT = [k.sb(f"pT{h}", [P, NR, BANK], F32R) for h in range(2)]
        oT = k.sb("oT", [P, 2, BANK])
        y_half = k.sb("y_half", [P, 2, G * HD])
        y_st = k.sb("y_st", [P, 2, G * HD])
        nmax = k.sb("nmax", [P, 2, 2, G])
        nrow = k.sb("nrow", [P, G])
        below = k.sb("below", [P, 2, G])
        scale = k.sb("scale", [P, 2, 2, G])
        den = k.sb("den", [P, 2, 2, G])
        dscaled = k.sb("dscaled", [P, 2, G])
        dsum = k.sb("dsum", [P, G])
        rden = k.sb("rden", [P, G])
        factor = k.sb("factor", [P, 2, 2, G])
        score = ctx.enter_context(nc.psum_tensor("mixa_score", [P, 4 * BANK], F32))
        turned = [ctx.enter_context(nc.psum_tensor(f"mixa_turned{i}", [P, BANK], F32)) for i in range(2)]
        out_acc = [ctx.enter_context(nc.psum_tensor(f"mixa_out_acc{i}", [P, BANK], F32)) for i in range(2)]
        turn_banks = [turned[0][:], turned[1][:]] + [score[:, i * BANK:(i + 1) * BANK] for i in range(4)]

        fold_in = k.sem("fold_in")
        const_in, k_in, v_dma, q_dma = k.sem("const_in"), k.sems("k_in", NT // 4), k.sem("v_dma"), k.sem("q_dma")
        kt_done, kt_hi, kt_lo = k.sem("kt_done"), k.sem("kt_hi"), k.sem("kt_lo")
        v_hi, v_lo = k.sem("v_hi"), k.sem("v_lo")
        qt_done, qt_hi, qt_lo = k.sem("qt_done"), k.sem("qt_hi"), k.sem("qt_lo")
        sc_done, nm_done, exp_done = (k.sem(n) for n in ("sc_done", "nm_done", "exp_done"))
        t_done, hi_done, lo_done, pv_done = (k.sem(n) for n in ("t_done", "hi_done", "lo_done", "pv_done"))
        row_done, merge, scale_done, recip_done = k.sem("row_done"), k.sem("merge"), k.sem("scale_done"), k.sem("recip_done")
        o_done, fold_done, half_done, y_done = (k.sem(n) for n in ("o_done", "fold_done", "half_done", "y_done"))
        y_out = k.sems("y_out", 2)
        rows_out = k.sem("rows_out")
        set_done = k.sem("set_done")
        MERGE = 4
        block = ctx.enter_context(nc.Block())


        @block.sync
        def _(sp):
            sp.dma_start(q_in[:], scr["qA"][0:P, :]).then_inc(q_dma, 16)
            sp.dma_start(ident[:], ident_d).then_inc(const_in, 16)
            for j in range(NT // 4):
                sp.dma_start(k_raw[:, 4 * j:4 * j + 4, :], scr["kA"][j * BT:(j + 1) * BT, :].rearrange(
                    "(j p) c -> p j c", p=P)).then_inc(k_in[j], 16)
            sp.dma_start(v_raw[:], scr["vA"].rearrange("(j p) c -> p j c", p=P)).then_inc(v_dma, 16)
            sp.dma_start(fold[:], fold_d).then_inc(fold_in, 16)
            sp.wait_ge(qt_done, 2)
            sp.dma_start(q_in[:], scr["qA"][P:2 * P, :]).then_inc(q_dma, 16)

            def store(g, row, count):
                sp.wait_ge(y_done, count)
                sp.dma_start(scr["yA"][row, g * G * HD:(g + 1) * G * HD], y_st[:, g, :]).then_inc(y_out[g], 16)

            def one(it, tile):
                store(1, bass.ds(it * P, P), it * 2 + 1)
                store(0, bass.ds(it * P + P, P), it * 2 + 2)
                sp.wait_ge(qt_done, it * 2 + 4)
                sp.dma_start(q_in[:], scr["qA"][tile, :]).then_inc(q_dma, 16)

            def bias_rows(h):
                a, to = scr["bias"][bass.ds(h, 1), :], scr["table"][bass.ds(h, 1), :, :].rearrange("h p n -> (h p) n")
                sp.dma_start(to, bass.AP(a.tensor, a.offset, [[0, P], [1, ROWS_W]])).then_inc(rows_out, 16)

            with sp.Fori(0, NHB) as it:
                one(it, bass.ds(it * P + 2 * P, P))
                bias_rows(it)
            with sp.Fori(NHB, NT - 2) as it:
                one(it, bass.ds(it * P + 2 * P, P))
            one(NT - 2, slice(0, P))
            one(NT - 1, slice(0, P))
            store(1, slice(NT * P, NT * P + P), 2 * NT + 1)
            sp.wait_ge(rows_out, 16 * NHB)
            sp.wait_ge(y_out[0], 16 * (NT + 1))
            sp.wait_ge(y_out[1], 16 * (NT + 2))
            sp.wait_ge(q_dma, 16 * (NT + 2))

        @block.gpsimd
        def _(pool):
            pool.memset(pT[0][:, 2:4, :].bitcast(F32), 0.0).then_inc(set_done, 1)
            pool.memset(pT[1][:, 2:4, :].bitcast(F32), 0.0).then_inc(set_done, 1)
            pool.memset(factor[:], 0.0).then_inc(set_done, 1)
            pool.memset(y_half[:], 0.0).then_inc(set_done, 1)
            pool.sem_inc(pv_done, 2)
            pool.sem_inc(lo_done, 2)
            pool.sem_inc(half_done, 1)
            for s in y_out:
                pool.sem_inc(s, 16)

            def merged(U, w):
                pool.wait_ge(exp_done, U * NC + NC)
                pool.wait_ge(row_done, U + 1)
                pool.tensor_tensor(below[:], nrow[:].unsqueeze(1).broadcast_to([P, 2, G]), nmax[:, w, :, :],
                                   ALU.subtract).then_inc(merge, 1)
                pool.wait_ge(scale_done, U + 1)
                pool.tensor_tensor(dscaled[:], den[:, w, :, :], scale[:, w, :, :], ALU.mult).then_inc(merge, 1)
                pool.wait_ge(merge, U * MERGE + 2)
                pool.tensor_tensor(dsum[:], dscaled[:, 0, :], dscaled[:, 1, :], ALU.add).then_inc(merge, 1)
                pool.wait_ge(recip_done, U + 1)
                pool.tensor_tensor(factor[:, w, :, :], scale[:, w, :, :], rden[:].unsqueeze(1).broadcast_to([P, 2, G]),
                                   ALU.mult).then_inc(merge, 1)

            def summed(count, slot, stored):
                pool.wait_ge(half_done, count * 2)
                pool.wait_ge(y_out[slot], stored)
                pool.tensor_tensor(y_st[:, slot, :], y_half[:, 0, :], y_half[:, 1, :], ALU.add).then_inc(y_done, 1)

            with pool.Fori(0, NT) as it:
                for w in range(2):
                    U = it * 2 + w
                    merged(U, w)
                    summed(U + 1, 1 - w, it * 16 + 16)
            summed(2 * NT + 1, 1, 16 * NT + 16)

        @block.tensor
        def _(pe):
            def turn_queries(V, g, bank, first=False):
                pe.wait_ge(q_dma, (V - g) * 8 + 16)
                if not first:
                    pe.wait_ge(half_done, V * 2 - 2)
                for h in range(G):
                    mm = pe.transpose(bank[:, h * P:(h + 1) * P], q_in[:, (G * g + h) * P:(G * g + h + 1) * P], ident[:])
                mm.then_inc(qt_done, 1)

            def scores(V, g, c):
                half, h = c // G, c % G
                if c == 0:
                    pe.wait_ge(qt_lo, V + 1)
                if not (isinstance(V, int) and c < 2):
                    pe.wait_ge(exp_done, V * NC + c - 1)
                for j in range(2):
                    kc = 2 * half + j
                    at = 2 * (c % 2) + j
                    for part in range(2):
                        mm = pe.matmul(score[:, at * BANK:(at + 1) * BANK], qT[g][:, h, :],
                                       kT[g][part][:, kc * BANK:(kc + 1) * BANK], start=part == 0, stop=part == 1)
                mm.then_inc(sc_done, 1)

            def values(U, g, s):
                half = s // (NT // 2)
                pe.wait_ge(lo_done, U * NT + s + 3)
                if s == 0:
                    pe.wait_ge(half_done, U * 2 + 1)
                if s == NT // 2:
                    pe.wait_ge(qt_lo, U + 3)
                for part in range(2):
                    mm = pe.matmul(out_acc[half][:], v_hl[:, s, g, :], pT[part][:, s % NR, :],
                                   start=s % (NT // 2) == 0 and part == 0,
                                   stop=s % (NT // 2) == NT // 2 - 1 and part == 1)
                mm.then_inc(pv_done, 1)

            def fold_out(count, half):
                pe.wait_ge(o_done, count)
                for h in range(G):
                    mm = pe.matmul(out_acc[half][:, h * HD:(h + 1) * HD], oT[:, half, h * P:(h + 1) * P], fold[:],
                                   start=True, stop=True)
                mm.then_inc(fold_done, 1)

            pe.wait_ge(const_in, 16)
            pe.wait_ge(q_dma, 16)
            turn_queries(0, 0, out_acc[0], True)
            turn_queries(1, 1, out_acc[1], True)
            for n in range(2 * NT // 4):
                g, j0 = n % 2, 4 * (n // 2)
                if g == 0:
                    pe.wait_ge(k_in[n // 2], 16)
                if n >= 6:
                    pe.wait_ge(kt_lo, n - 5)
                for j in range(4):
                    mm = pe.transpose(turn_banks[n % 6][:, j * P:(j + 1) * P], k_raw[:, j0 + j, g * P:(g + 1) * P],
                                      ident[:])
                mm.then_inc(kt_done, 1)
            pe.wait_ge(kt_lo, 6)
            for c in range(NC):
                scores(0, 0, c)
            pe.wait_ge(kt_lo, 2 * NT // 4)
            pe.wait_ge(v_lo, 1)
            pe.wait_ge(fold_in, 16)
            pe.wait_ge(set_done, 4)
            pe.wait_ge(qt_lo, 2)
            pe.matmul(out_acc[1][:], v_hl[:, NT - 3, 1, :], pT[0][:, 2, :], start=True, stop=False)
            with pe.Fori(0, NT) as it:
                for w in range(2):
                    U = it * 2 + w
                    for s in range(NT):
                        if s in (0, NT // 2):
                            pe.wait_ge(exp_done, U * NC + (G if s == 0 else NC))
                        pe.wait_ge(lo_done, U * NT + s + 1)
                        for h in range(G):
                            mm = pe.transpose(turned[s % 2][:, h * P:(h + 1) * P], prob[w][:, h, s * P:(s + 1) * P],
                                              ident[:])
                        mm.then_inc(t_done, 1)
                        if s < 2:
                            values(U - 1, 1 - w, s + NT - 2)
                        else:
                            values(U, w, s - 2)
                        if s % 2 == 0:
                            scores(U + 1, 1 - w, s // 2)
                        if s == 4:
                            fold_out(U * 2 + 1, 1)
                        if s == 6:
                            turn_queries(U + 2, w, out_acc[1])
                        if s == 12:
                            fold_out(U * 2 + 2, 0)
            values(2 * NT - 1, 1, NT - 2)
            values(2 * NT - 1, 1, NT - 1)
            fold_out(4 * NT + 1, 1)

        @block.scalar
        def _(act):
            def query_hi(V, g, bank):
                act.wait_ge(qt_done, V + 1)
                act.activation(qT[g][:].rearrange("p h n -> p (h n)"), bank[:], ACT.Copy).then_inc(qt_hi, 1)

            def exponential(V, par, c):
                half, h = c // G, c % G
                act.wait_ge(nm_done, V * NC + c + 1)
                act.activation(prob[par][:, h, half * 2 * BANK:(half + 1) * 2 * BANK],
                               score[:, 2 * (c % 2) * BANK:2 * (c % 2 + 1) * BANK], ACT.Exp,
                               bias=nmax[:, par, half, h:h + 1], accum_out=den[:, par, half, h:h + 1]
                               ).then_inc(exp_done, 1)

            def sums_out(U, half):
                act.wait_ge(pv_done, U * NT + (half + 1) * NT // 2 + 4)
                act.activation(oT[:, half, :], out_acc[half][:], ACT.Copy).then_inc(o_done, 1)

            query_hi(0, 0, out_acc[0])
            query_hi(1, 1, out_acc[1])
            for n in range(2 * NT // 4):
                act.wait_ge(kt_done, n + 1)
                act.activation(kT[n % 2][0][:, (n // 2) * BANK:(n // 2 + 1) * BANK], turn_banks[n % 6], ACT.Copy
                               ).then_inc(kt_hi, 1)
            for c in range(NC - 1):
                exponential(0, 0, c)
                if c == G:
                    act.wait_ge(v_dma, 16)
                    act.activation(v_hl[:, :, :, 0:HD], v_raw[:].rearrange("p j (g d) -> p j g d", g=NKV), ACT.Copy
                                   ).then_inc(v_hi, 1)
            with act.Fori(0, NT) as it:
                for w in range(2):
                    U = it * 2 + w
                    for s in range(NT):
                        act.wait_ge(t_done, U * NT + s + 1)
                        act.wait_ge(pv_done, U * NT + s + 1)
                        act.activation(pT[0][:, s % NR, :], turned[s % 2][:], ACT.Copy).then_inc(hi_done, 1)
                        if s == 0:
                            exponential(U, w, NC - 1)
                        elif s % 2 == 0:
                            exponential(U + 1, 1 - w, s // 2 - 1)
                        if s == 3:
                            sums_out(U - 1, 1)
                            act.wait_ge(merge, U * MERGE + 1)
                            act.activation(scale[:, w, :, :], below[:], ACT.Exp).then_inc(scale_done, 1)
                        if s == 7:
                            query_hi(U + 2, w, out_acc[1])
                        if s == 11:
                            sums_out(U, 0)
            sums_out(2 * NT - 1, 1)

        @block.vector
        def _(ve):
            def query_lo(V, g, bank):
                ve.wait_ge(qt_hi, V + 1)
                lower = qT[g][HD:P, :, :].rearrange("p h n -> p (h n)")
                ve.tensor_tensor(lower, bank[HD:P, :], lower.bitcast(F32), ALU.subtract).then_inc(qt_lo, 1)

            def maximum(V, par, c):
                ve.wait_ge(sc_done, V * NC + c + 1)
                ve.tensor_reduce(nmax[:, par, c // G, c % G:c % G + 1], score[:, 2 * (c % 2) * BANK:
                                                                             2 * (c % 2 + 1) * BANK],
                                 AXX, ALU.max, negate=True).then_inc(nm_done, 1)

            def output(count, slot, half):
                ve.wait_ge(fold_done, count)
                ve.tensor_tensor(y_half[:, half, :].rearrange("p (h d) -> p h d", h=G),
                                 out_acc[half][:, 0:G * HD].rearrange("p (h d) -> p h d", h=G),
                                 factor[:, slot, half, :].unsqueeze(2).broadcast_to([P, G, HD]), ALU.mult
                                 ).then_inc(half_done, 1)

            query_lo(0, 0, out_acc[0])
            query_lo(1, 1, out_acc[1])
            for n in range(2 * NT // 4):
                at = slice((n // 2) * BANK, (n // 2 + 1) * BANK)
                ve.wait_ge(kt_hi, n + 1)
                ve.tensor_tensor(kT[n % 2][1][:, at], turn_banks[n % 6], kT[n % 2][0][:, at].bitcast(F32),
                                 ALU.subtract).then_inc(kt_lo, 1)
            for c in range(NC):
                maximum(0, 0, c)
            ve.wait_ge(v_hi, 1)
            ve.tensor_tensor(v_hl[:, :, :, HD:2 * HD], v_raw[:].rearrange("p j (g d) -> p j g d", g=NKV),
                             v_hl[:, :, :, 0:HD].bitcast(F32), ALU.subtract).then_inc(v_lo, 1)
            with ve.Fori(0, NT) as it:
                for w in range(2):
                    U = it * 2 + w
                    for s in range(NT):
                        ve.wait_ge(hi_done, U * NT + s + 1)
                        ve.tensor_tensor(pT[1][:, s % NR, :], turned[s % 2][:], pT[0][:, s % NR, :].bitcast(F32),
                                         ALU.subtract).then_inc(lo_done, 1)
                        if s % 2 == 0:
                            maximum(U + 1, 1 - w, s // 2)
                        if s == 1:
                            ve.wait_ge(nm_done, U * NC + NC)
                            ve.tensor_tensor(nrow[:], nmax[:, w, 0, :], nmax[:, w, 1, :], ALU.min).then_inc(row_done, 1)
                        if s == 5:
                            output(U * 2 + 1, 1 - w, 1)
                            ve.wait_ge(merge, U * MERGE + 3)
                            ve.reciprocal(rden[:], dsum[:]).then_inc(recip_done, 1)
                        if s == 7:
                            query_lo(U + 2, w, out_acc[1])
                        if s == 13:
                            ve.wait_ge(merge, U * MERGE + 4)
                            ve.wait_ge(y_done, U + 1)
                            output(U * 2 + 2, w, 0)
            output(4 * NT + 1, 1, 1)


def mixer_b_phase(nc, ident_d, fold_d, scr, step):
    NU = 16
    NK = 8
    VT = NU + RES
    SW = S + 2 * PAD
    SLOTS = 4
    with ExitStack() as ctx:
        k = Kit(nc, ctx, "mixb")
        ident = k.sb("ident", [P, P])
        fold = k.sb("fold", [P, HD])
        q_in = k.sb("q_in", [P, NU, 2 * HD])
        k_in = k.sb("k_in", [P, NU, 2 * HD])
        v_in = k.sb("v_in", [P, VT, HD])
        kT = [[k.sb(f"kT{u}{h}", [P, SW], F32R) for h in range(2)] for u in range(2)]
        qT = [k.sb(f"qT{u}", [P, S], F32R) for u in range(2)]
        v_hl = [k.sb(f"v_hl{u}", [P, VT, 2 * HD], F32R) for u in range(2)]
        t_own = [k.sb(f"t_own{u}", [P, 7 * P]) for u in range(2)]
        t_oth = [k.sb(f"t_oth{u}", [P, 6, P]) for u in range(2)]
        t_near = k.sb("t_near", [P, TABLE_W - OWN_W])
        t_end = [k.sb(f"t_end{u}", [P, 3, RES, RES, 2, PAD]) for u in range(2)]
        prob = k.sb("prob", [P, SLOTS, 2 * BANK])
        pT = k.sb("pT", [P, 2, NK, 2, P], F32R)
        pre = k.sb("pre", [P, 2, BANK])
        pmax = k.sb("pmax", [P, SLOTS, 3])
        nmax = k.sb("nmax", [P, SLOTS])
        den = k.sb("den", [P, SLOTS])
        rden = k.sb("rden", [P, SLOTS])
        oT = k.sb("oT", [P, 2, 2 * P])
        y_st = k.sb("y_st", [P, 2, NU, HD])
        score = [ctx.enter_context(nc.psum_tensor(f"mixb_score{i}", [P, 2 * BANK], F32)) for i in range(2)]
        turned = [ctx.enter_context(nc.psum_tensor(f"mixb_turned{i}", [P, BANK], F32)) for i in range(2)]
        out_acc = [ctx.enter_context(nc.psum_tensor(f"mixb_out_acc{i}", [P, BANK], F32)) for i in range(2)]

        pre_banks = [out_acc[0][:], out_acc[1][:]] + [score[i // 2][:, i % 2 * BANK:(i % 2 + 1) * BANK] for i in range(4)]

        const_in, fold_in, set_done = k.sem("const_in"), k.sem("fold_in"), k.sem("set_done")
        qk_dma, v_dma, t_dma = k.sem("qk_dma"), k.sem("v_dma"), k.sem("t_dma")
        t_done_pool = k.sem("t_done_pool")
        pre_done, pre_raw, pre_hi, pre_lo, v_hi, v_lo = (k.sem(n) for n in ("pre_done", "pre_raw", "pre_hi", "pre_lo",
                                                                            "v_hi", "v_lo"))
        sc_done, add_done, nm_done, exp_done = (k.sem(n) for n in ("sc_done", "add_done", "nm_done", "exp_done"))
        t_done, hi_done, lo_done, pv_done = (k.sem(n) for n in ("t_done", "hi_done", "lo_done", "pv_done"))
        rd_done, o_done, fold_done, y_done = (k.sem(n) for n in ("rd_done", "o_done", "fold_done", "y_done"))
        y_out = k.sems("y_out", 2)
        QK_DMAS, V_DMAS = 2, 1 + 2 * RES
        T_COPIES = 2 + 3 * RES
        PRE = 8
        block = ctx.enter_context(nc.Block())

        first_tile = lambda n: int(n % RES in (0, RES - 1))
        first_own = lambda n: int(n % RES == RES - 1)

        @block.sync
        def _(sp):
            def copies(name, h):
                a = scr[name][:, bass.ds(h * 2 * HD, 2 * HD)]
                return bass.AP(a.tensor, a.offset, [[2 * D_AB, P], [2 * P * D_AB, NU], [1, 2 * HD]])

            def load_qk(h):
                sp.dma_start(q_in[:], copies("qB", h)).then_inc(qk_dma, 16)
                sp.dma_start(k_in[:], copies("kB", h)).then_inc(qk_dma, 16)

            def load_v(h):
                sp.dma_start(v_in[:, 0:NU, :], scr["vB"][PAD:PAD + S, bass.ds(h * HD, HD)].rearrange(
                    "(j p) c -> p j c", p=P)).then_inc(v_dma, 16)
                for r in range(RES):
                    for side in range(2):
                        row = r * SUB + side * (P + PAD)
                        a = scr["vB"][row:row + PAD, bass.ds(h * HD, HD)]
                        sp.dma_start(v_in[(2 * r + side) * PAD:(2 * r + side + 1) * PAD, NU:VT, :],
                                     bass.AP(a.tensor, a.offset, [[D_AB, PAD], [P * D_AB, RES], [1, HD]])
                                     ).then_inc(v_dma, 16)

            def load_near(h):
                a = scr["table"][bass.ds(h, 1), :, :]
                sp.dma_start(t_near[:].rearrange("p (v n) -> p v n", v=7),
                             bass.AP(a.tensor, a.offset + OWN_W + 2 * P - 1,
                                     [[ROWS_W - 1, P], [P + 2 * PAD + P, 7], [1, P + 2 * PAD]])).then_inc(t_dma, 16)

            def load_own(h, par):
                a = scr["table"][bass.ds(h, 1), :, :]
                sp.dma_start(t_own[par][:], bass.AP(a.tensor, a.offset + P - 1, [[ROWS_W - 1, P], [1, OWN_W]])
                             ).then_inc(t_dma, 16)

            sp.dma_start(ident[:], ident_d).then_inc(const_in, 16)
            load_near(0)
            load_qk(0)
            load_own(0, 0)
            sp.dma_start(fold[:], fold_d).then_inc(fold_in, 16)
            load_v(0)

            def load_next(h, nxt):
                sp.wait_ge(pre_done, h * PRE + PRE)
                load_qk(nxt)
                sp.wait_ge(v_lo, h + 1)
                load_v(nxt)

            def next_tables(h, par, nxt):
                sp.wait_ge(add_done, h * (3 * NU) + 6)
                sp.wait_ge(t_done_pool, h * T_COPIES + T_COPIES)
                load_near(nxt)
                load_own(nxt, 1 - par)

            def store(h, par):
                sp.wait_ge(y_done, h * NU + NU + 2)
                a = scr["yB"][:, bass.ds(h * HD, HD)]
                sp.dma_start(bass.AP(a.tensor, a.offset, [[D_AB, P], [P * D_AB, NU], [1, HD]]), y_st[:, par, :, :]
                             ).then_inc(y_out[par], 16)

            def one(h, par, nxt):
                load_next(h, nxt)
                next_tables(h, par, nxt)
                store(h - 1, 1 - par)

            load_next(0, 1)
            next_tables(0, 0, 1)
            with sp.Fori(0, NHB // 2 - 1) as it:
                for u in range(2):
                    one(it * 2 + 1 + u, 1 - u, it * 2 + 2 + u)
            one(NHB - 1, 1, 0)
            store(NHB - 1, 1)
            for s in y_out:
                sp.wait_ge(s, 16 * (NHB // 2 + 1))
            sp.wait_ge(t_dma, 32 * (NHB + 1))
            sp.wait_ge(qk_dma, 16 * QK_DMAS * (NHB + 1))
            sp.wait_ge(v_dma, 16 * V_DMAS * (NHB + 1))

        @block.gpsimd
        def _(pool):
            for u in range(2):
                for h in range(2):
                    pool.memset(kT[u][h][:, 0:PAD].bitcast(F32), 0.0)
                    pool.memset(kT[u][h][:, PAD + S:SW].bitcast(F32), 0.0).then_inc(set_done, 1)
                pool.memset(t_end[u][:], NEG).then_inc(set_done, 1)
            for s in y_out:
                pool.sem_inc(s, 16)
            pool.memset(oT[:, 1, :], 0.0).then_inc(set_done, 1)
            pool.memset(rden[:, SLOTS - 1:SLOTS], 0.0).then_inc(set_done, 1)
            pool.sem_inc(o_done, 1)
            pool.sem_inc(y_done, 1)

            def tables(par):
                near = t_near[:].rearrange("p (v n) -> p v n", v=7)
                for i, v in enumerate((0, 4)):
                    pool.tensor_copy(t_oth[par][:, 3 * i:3 * i + 3, :], near[:, v:v + 3, PAD:PAD + P]
                                     ).then_inc(t_done_pool, 1)
                for r in range(RES):
                    a = near[:, 3 - r:7 - r, 0:PAD]
                    both = bass.AP(a.tensor, a.offset, [[TABLE_W - OWN_W, P], [P + 2 * PAD, RES], [P + PAD, 2],
                                                        [1, PAD]])
                    pool.tensor_copy(t_end[par][:, 1, r, :, :, :], both).then_inc(t_done_pool, 1)
                    pool.tensor_copy(t_end[par][:, 0, r, :, 1, :], near[:, 3 - r:7 - r, PAD + P:2 * PAD + P]
                                     ).then_inc(t_done_pool, 1)
                    pool.tensor_copy(t_end[par][:, 2, r, :, 0, :], near[:, 3 - r:7 - r, 0:PAD]
                                     ).then_inc(t_done_pool, 1)

            pool.wait_ge(set_done, 8)
            pool.wait_ge(t_dma, 32)
            tables(0)
            def split_pre(h, par, m):
                raw = pre[:, m % 2, :]
                pool.wait_ge(pre_raw, (h - 1) * PRE + (m + 1))
                pool.sem_inc(step, 1)
                at = slice(PAD * (m >= 4) + m % 4 * BANK, PAD * (m >= 4) + (m % 4 + 1) * BANK)
                hi = (qT[par] if m < 4 else kT[par][0])[:, at]
                pool.tensor_scalar(hi, raw, 1.0, 0.0, ALU.mult, ALU.add).then_inc(pre_hi, 1)
                pool.wait_ge(pre_hi, h * PRE + m + 1)
                if m < 4:
                    low = qT[par][HD:P, at]
                    pool.tensor_tensor(low, raw[HD:P, :], low.bitcast(F32), ALU.subtract).then_inc(pre_lo, 1)
                    pool.wait_ge(pre_lo, h * PRE + m + 1)
                else:
                    pool.tensor_tensor(kT[par][1][:, at], raw, hi.bitcast(F32), ALU.subtract).then_inc(pre_lo, 1)

            def split_values(h, par):
                pool.wait_ge(v_dma, h * (16 * V_DMAS) + 16 * V_DMAS)
                pool.sem_inc(step, 1)
                pool.tensor_scalar(v_hl[par][:, :, 0:HD], v_in[:], 1.0, 0.0, ALU.mult, ALU.add).then_inc(v_hi, 1)
                pool.wait_ge(v_hi, h + 1)
                pool.tensor_tensor(v_hl[par][:, :, HD:2 * HD], v_in[:], v_hl[par][:, :, 0:HD].bitcast(F32), ALU.subtract
                                   ).then_inc(v_lo, 1)

            with pool.Fori(0, NHB // 2) as it:
                for par in range(2):
                    h = it * 2 + par
                    for m in range(PRE):
                        split_pre(h + 1, 1 - par, m)
                    split_values(h + 1, 1 - par)
                    pool.wait_ge(t_dma, h * 32 + 64)
                    pool.wait_ge(add_done, h * (3 * NU) + 6)
                    pool.sem_inc(step, 1)
                    tables(1 - par)

        def others(r):
            return [x for x in range(RES) if x != r]

        @block.tensor
        def _(pe):
            def prepare(h, m):
                if m == 0:
                    pe.wait_ge(qk_dma, h * (16 * QK_DMAS) + 16 * QK_DMAS)
                first = isinstance(h, int)
                if first and m >= 6:
                    pe.wait_ge(pre_lo, m - 5)
                src = q_in if m < 4 else k_in
                for j in range(4):
                    mm = pe.transpose(pre_banks[m % (6 if first else 2)][:, j * P:(j + 1) * P],
                                      src[:, 4 * (m % 4) + j, :], ident[:])
                mm.then_inc(pre_done, 1)

            def scores(N, par, n):
                r, b = n // RES, n % RES
                if not (isinstance(N, int) and N < 2):
                    pe.wait_ge(add_done, N * 3 - 3)
                sc = score[n % 2]
                q = qT[par][:, n * P:(n + 1) * P]
                for part in range(2):
                    kt = kT[par][part]
                    main = kt[:, PAD:PAD + S].rearrange("p (r m) -> p r m", r=RES)
                    own = first_own(n)
                    pe.matmul(sc[:, first_tile(n) * P:BANK], q, main[:, r, own * P:(own + RES - first_tile(n)) * P],
                              start=part == 0, stop=part == 1)
                at = BANK
                runs = [x for x in ((0, r), (r + 1, RES)) if x[1] > x[0]]
                for a, z in runs:
                    for part in range(2):
                        main = kT[par][part][:, PAD:PAD + S].rearrange("p (r m) -> p r m", r=RES)
                        pe.matmul(sc[:, at:at + (z - a) * P], q, main[:, a:z, b * P:(b + 1) * P],
                                  start=part == 0, stop=part == 1)
                    at += (z - a) * P
                for part in range(2):
                    t = kT[par][part][:, b * P:b * P + PAD]
                    ends = bass.AP(t.tensor, t.offset, [[SW, P], [SUB, RES], [P + PAD, 2], [1, PAD]])
                    mm = pe.matmul(sc[:, at:at + P], q, ends, start=part == 0, stop=part == 1)
                mm.then_inc(sc_done, 1)

            def turn(N, n):
                pe.wait_ge(exp_done, N + 1)
                for half in range(2):
                    if not (isinstance(N, int) and N == 0):
                        pe.wait_ge(lo_done, N * 2 + half - 1)
                    for j in range(0 if half else first_tile(n), 4):
                        c = 4 * half + j
                        mm = pe.transpose(turned[half][:, j * P:(j + 1) * P], prob[:, n % SLOTS, c * P:(c + 1) * P],
                                          ident[:])
                    mm.then_inc(t_done, 1)

            def values(N, h, par, n):
                r, b = n // RES, n % RES
                c0 = first_tile(n)
                tiles = ([RES * r + first_own(n) + j for j in range(RES - c0)] + [RES * x + b for x in others(r)] +
                         [NU + b])
                pe.wait_ge(lo_done, N * 2 + 2)
                pe.wait_ge(y_done, N + 1)
                if 2 <= n < 2 + PRE:
                    pe.wait_ge(pre_raw, h * PRE + (n - 1))
                for c, vt in enumerate(tiles, c0):
                    mm = pe.matmul(out_acc[n % 2][:, 0:2 * P], v_hl[par][:, vt, :],
                                   pT[:, n % 2, c, :, :].rearrange("p h n -> p (h n)"), start=c == c0, stop=c == NK - 1)
                mm.then_inc(pv_done, 1)

            def fold_out(count, n):
                pe.wait_ge(o_done, count)
                for part in range(2):
                    mm = pe.matmul(out_acc[n % 2][:, 0:HD], oT[:, n % 2, part * P:(part + 1) * P], fold[:],
                                   start=part == 0, stop=part == 1)
                mm.then_inc(fold_done, 1)

            pe.wait_ge(const_in, 16)
            for m in range(PRE):
                prepare(0, m)
            pe.wait_ge(fold_in, 16)
            pe.wait_ge(set_done, 8)
            pe.wait_ge(pre_lo, PRE)
            scores(0, 0, 0)
            scores(1, 0, 1)
            pe.wait_ge(v_lo, 1)
            turn(0, 0)
            with pe.Fori(0, NHB // 2) as it:
                for par in range(2):
                    h = it * 2 + par
                    for n in range(NU):
                        N = h * NU + n
                        if 2 <= n < 2 + PRE:
                            pe.wait_ge(y_done, N + 1)
                            prepare(h + 1, n - 2)
                        if n < NU - 2:
                            scores(N + 2, par, n + 2)
                        else:
                            if n == NU - 2:
                                pe.wait_ge(pre_lo, h * PRE + 2 * PRE)
                                pe.wait_ge(v_lo, h + 2)
                            scores(N + 2, 1 - par, n + 2 - NU)
                        turn(N + 1, (n + 1) % NU)
                        fold_out(N + 1, n - 1)
                        values(N, h, par, n)
            fold_out(NHB * NU + 1, NU - 1)

        @block.scalar
        def _(act):
            def pre_hi_part(h, par, m):
                act.wait_ge(pre_done, h * PRE + m + 1)
                dst = qT[par][:, m * BANK:(m + 1) * BANK] if m < 4 else kT[par][0][:, PAD + (m - 4) * BANK:
                                                                               PAD + (m - 3) * BANK]
                act.activation(dst, pre_banks[m % 6], ACT.Copy).then_inc(pre_hi, 1)

            def pre_out(h, m):
                act.wait_ge(pre_done, h * PRE + m + 1)
                act.wait_ge(pre_lo, h * PRE + m - 1)
                act.activation(pre[:, m % 2, :], out_acc[m % 2][:], ACT.Copy).then_inc(pre_raw, 1)

            def value_hi(h, par):
                act.wait_ge(v_dma, h * (16 * V_DMAS) + 16 * V_DMAS)
                act.activation(v_hl[par][:, :, 0:HD], v_in[:], ACT.Copy).then_inc(v_hi, 1)

            def exponential(N, n):
                act.wait_ge(nm_done, N + 1)
                p = prob[:, n % SLOTS, first_tile(n) * P:]
                act.activation(p, p, ACT.Exp, bias=nmax[:, n % SLOTS:n % SLOTS + 1],
                               accum_out=den[:, n % SLOTS:n % SLOTS + 1]).then_inc(exp_done, 1)

            def turned_hi(N, n):
                for half in range(2):
                    act.wait_ge(t_done, N * 2 + half + 1)
                    j = 0 if half else first_tile(n)
                    act.activation(pT[:, n % 2, 4 * half + j:4 * half + 4, 0, :],
                                   turned[half][:, j * P:].rearrange("p (c n) -> p c n", n=P), ACT.Copy
                                   ).then_inc(hi_done, 1)

            def sums_out(N, n):
                act.wait_ge(pv_done, N + 1)
                act.activation(oT[:, n % 2, :], out_acc[n % 2][:, 0:2 * P], ACT.Copy).then_inc(o_done, 1)

            for m in range(PRE):
                pre_hi_part(0, 0, m)
            exponential(0, 0)
            value_hi(0, 0)
            exponential(1, 1)
            turned_hi(0, 0)
            with act.Fori(0, NHB // 2) as it:
                for par in range(2):
                    h = it * 2 + par
                    for n in range(NU):
                        N = h * NU + n
                        turned_hi(N + 1, n + 1)
                        exponential(N + 2, n + 2)
                        if 1 <= n < 1 + PRE:
                            pre_out(h + 1, n - 1)
                        sums_out(N, n)

        @block.vector
        def _(ve):
            def pre_lo_part(h, par, m):
                ve.wait_ge(pre_hi, h * PRE + m + 1)
                if m < 4:
                    at = slice(m * BANK, (m + 1) * BANK)
                    low = qT[par][HD:P, at]
                    ve.tensor_tensor(low, pre_banks[m % 6][HD:P, :], low.bitcast(F32), ALU.subtract).then_inc(pre_lo, 1)
                else:
                    at = slice(PAD + (m - 4) * BANK, PAD + (m - 3) * BANK)
                    ve.tensor_tensor(kT[par][1][:, at], pre_banks[m % 6], kT[par][0][:, at].bitcast(F32), ALU.subtract
                                     ).then_inc(pre_lo, 1)

            def value_lo(h, par):
                ve.wait_ge(v_hi, h + 1)
                ve.tensor_tensor(v_hl[par][:, :, HD:2 * HD], v_in[:], v_hl[par][:, :, 0:HD].bitcast(F32), ALU.subtract
                                 ).then_inc(v_lo, 1)

            def add_bias(N, par, n):
                r, b = n // RES, n % RES
                edge = 0 if b == 0 else 2 if b == RES - 1 else 1
                sc, slot = score[n % 2], n % SLOTS
                c0, own = first_tile(n), first_own(n)
                parts = ((c0 * P, BANK, t_own[par][:, (3 - b + own) * P:(7 - b + own - c0) * P]),
                         (BANK, BANK + 3 * P, t_oth[par][:, 3 - r:6 - r, :].rearrange("p a n -> p (a n)")),
                         (BANK + 3 * P, 2 * BANK, t_end[par][:, edge, r, :, :, :].rearrange("p a s n -> p (a s n)")))
                ve.wait_ge(sc_done, N + 1)
                ve.sem_inc(step, 1)
                for i, (a, z, table) in enumerate(parts):
                    ve.tensor_tensor_reduce(prob[:, slot, a:z], sc[:, a:z], table, 1.0, -3.0e38, ALU.add, ALU.max,
                                            pmax[:, slot, i:i + 1]).then_inc(add_done, 1)
                ve.wait_ge(add_done, N * 3 + 3)
                ve.tensor_reduce(nmax[:, slot:slot + 1], pmax[:, slot, :], AXX, ALU.max, negate=True).then_inc(nm_done, 1)

            def turned_lo(N, n):
                for half in range(2):
                    j = 0 if half else first_tile(n)
                    at = pT[:, n % 2, 4 * half + j:4 * half + 4, :, :]
                    ve.wait_ge(hi_done, N * 2 + half + 1)
                    ve.tensor_tensor(at[:, :, 1, :], turned[half][:, j * P:].rearrange("p (c n) -> p c n", n=P),
                                     at[:, :, 0, :].bitcast(F32), ALU.subtract).then_inc(lo_done, 1)

            def sums(N, n):
                ve.wait_ge(exp_done, N + 1)
                ve.reciprocal(rden[:, n % SLOTS:n % SLOTS + 1], den[:, n % SLOTS:n % SLOTS + 1]).then_inc(rd_done, 1)

            def output(count, par, n):
                ve.wait_ge(fold_done, count)
                ve.tensor_scalar(y_st[:, par, n, :], out_acc[n % 2][:, 0:HD], rden[:, n % SLOTS:n % SLOTS + 1], None, ALU.mult
                                 ).then_inc(y_done, 1)

            for m in range(PRE):
                pre_lo_part(0, 0, m)
            ve.wait_ge(t_dma, 32)
            ve.wait_ge(t_done_pool, T_COPIES)
            add_bias(0, 0, 0)
            add_bias(1, 0, 1)
            value_lo(0, 0)
            sums(0, 0)
            turned_lo(0, 0)
            with ve.Fori(0, NHB // 2) as it:
                for par in range(2):
                    h = it * 2 + par
                    for n in range(NU):
                        N = h * NU + n
                        if n < NU - 2:
                            add_bias(N + 2, par, n + 2)
                        else:
                            if n == NU - 2:
                                ve.wait_ge(t_done_pool, h * T_COPIES + 2 * T_COPIES)
                            add_bias(N + 2, 1 - par, n + 2 - NU)
                        if n == 1:
                            ve.wait_ge(y_out[par], (h - par) * 8 + 16)
                        output(N + 1, par if n else 1 - par, (n - 1) % NU)
                        sums(N + 1, n + 1)
                        turned_lo(N + 1, n + 1)
            output(NHB * NU + 1, 1, NU - 1)


def feed_phase(nc, x, w_tail, gains, g_out, g_mlp_pre, g_ple, pT_d, ident_d, scr, out, step):
    CW = 1024
    NR4 = 4
    NF = 8
    GROUPS = D_FF // (NF * P)
    FF = [c for g in range(GROUPS) for c in
          [("f", g, j) for j in range(NF)] + [("g2", g, n, q) for n in range(2) for q in range(4)]]
    G1 = [("g1", 0, n, q) for n in range(2) for q in range(4)]
    G3 = [c for n in range(2) for c in [("g3", 0, n, q) for q in range(4)] + [("ple", 0, n, 0)]]
    NFF, NG1, NG3, NCHB = len(FF), len(G1), len(G3), len(FF) + len(G1) + len(G3)
    LOAD_Y = {4 + 8 * t: t for t in range(TT)}
    NORM_Y = {5 + 8 * t: t for t in range(TT)}
    TURN_Y = {8 + 8 * t: t for t in range(TT)}
    TURN_Z = {2: 0, 3: 1, 4: 2, 5: 3}
    TURN_X = {2: 0, 3: 1, 4: 2, 5: 3}
    SQUARES = ((1, 0), (1, 1), (1, 2), (2, 0), (2, 1), (1, 3), (2, 2), (2, 3))
    P_AT = 48
    with ExitStack() as ctx:
        k = Kit(nc, ctx, "feed")
        ident = k.sb("ident", [P, P])
        gate_in = k.sb("gate_in", [P, 3, KD])
        g_row = k.sb("g_row", [P, 2, D])
        y_in = k.sb("y_in", [P, D])
        xn = k.sb("xn", [P, 2, D])
        junk = k.sb("junk", [P, 2, D], mybir.dt.bfloat16)
        ssq = k.sb("ssq", [P, 12, 2])
        ms = k.sb("ms", [P, 12, 2])
        rec = k.sb("rec", [P, 12, 2])
        rstd = k.sb("rstd", [P, 12, 2])
        xT = [[k.sb(f"xT{u}{h}", [P, KD, BT], F32R) for h in range(2)] for u in range(2)]
        fT = [k.sb(f"fT{h}", [P, NF, BT], F32R) for h in range(2)]
        pT = [k.sb(f"pT{h}", [P, 2, BT], F32R) for h in range(2)]
        w_raw = k.sb("w_raw", [P, NR4, CW])
        w_sp = [k.sb(f"w_split{h}", [P, NSPL, CW], F32R) for h in range(2)]
        total = k.sb("total", [P, TT, D])
        res = k.sb("res", [P, TT, D])
        rl = k.sb("rl", [P, 2, BANK])
        fs = k.sb("fs", [P, 2, BANK])
        bank = k.banks()
        acc, tp, fb = bank[0:4], bank[4:6], bank[6:8]

        const_in = k.sem("const_in")
        w_dma = k.sems("w_dma", NR4)
        w_hi, w_lo, w_used = k.sem("w_hi"), k.sem("w_lo"), k.sem("w_used")
        y_dma, x_dma, h2_out, h2_in, out_dma = (k.sem("y_dma"), k.sems("x_dma", TT), k.sems("h2_out", TT),
                                                k.sems("h2_in", TT), k.sems("out_dma", TT))
        sq_done, var_done, rec_done, rt_done = (k.sem(n) for n in ("sq_done", "var_done", "rec_done", "rt_done"))
        xn_done, tp_done, hi_done, lo_done = (k.sem(n) for n in ("xn_done", "tp_done", "hi_done", "lo_done"))
        acc_done, ev_act, ev_dve = k.sem("acc_done"), k.sem("ev_act"), k.sem("ev_dve")
        f_done, f_relu, f_hi, f_mul, f_lo = (k.sem(n) for n in ("f_done", "f_relu", "f_hi", "f_mul", "f_lo"))
        p_hi, p_lo = k.sem("p_hi"), k.sem("p_lo")
        gained, h_done = k.sem("gained"), k.sem("h_done")
        ple_done, prod_done, o_done = (k.sem(n) for n in ("ple_done", "prod_done", "o_done"))
        block = ctx.enter_context(nc.Block())

        norm_at = lambda b: 12 + 20 * b
        turn_at = lambda b: 8 + 12 * b
        acc_at = lambda b: 8 + 48 * b
        act_at = lambda b: 8 + 24 * b
        dve_at = lambda b: 24 * b
        h_at = lambda b: 4 + 8 * b
        f_at = lambda b: 4 * NF * b

        def blocks(eng, body):
            with eng.Fori(0, NBLK // 2 - 1) as it:
                for u in range(2):
                    body(it * 2 + u, u)
            body(NBLK - 2, 0)
            body(NBLK - 1, 1, True)

        @block.sync
        def _(sp):
            def load_y(b, row, t):
                if t > 0:
                    sp.wait_ge(xn_done, turn_at(b) + t)
                else:
                    sp.wait_ge(p_lo, b + 1)
                sp.sem_inc(step, 1)
                sp.dma_start(y_in[:, 0:D_AB], scr["yA"][bass.ds(row + (P + t * P), P), :]).then_inc(y_dma, 16)
                sp.dma_start(y_in[:, D_AB:D], scr["yB"][bass.ds(row + t * P, P), :]).then_inc(y_dma, 16)

            def load_w(C, i, slot):
                sp.wait_ge(w_lo, C - NR4 + 1)
                sp.dma_start(w_raw[:, slot, :], w_tail[i]).then_inc(w_dma[slot], 16)

            def load_h2(b, t):
                sp.wait_ge(h_done, h_at(b) + (4 + t + 1))
                sp.wait_ge(h2_out[t], b * 16 + 16)
                sp.dma_start(total[:, t, :], scr["h2"][t * P:(t + 1) * P, :]).then_inc(h2_in[t], 16)

            def store_out(b, t):
                sp.wait_ge(o_done, b * 8 + (4 + t) + 3)
                sp.dma_start(out[bass.ds(b * BT + t * P, P), :], total[:, t, :]).then_inc(out_dma[t], 16)

            def first_y(t):
                sp.dma_start(total[:, t, 0:D_AB], scr["yA"][P + t * P:2 * P + t * P, :]).then_inc(out_dma[t], 16)
                sp.dma_start(total[:, t, D_AB:D], scr["yB"][t * P:(t + 1) * P, :]).then_inc(out_dma[t], 16)

            first_y(0)
            sp.dma_start(ident[:], ident_d).then_inc(const_in, 16)
            for i, g in enumerate((g_out, g_mlp_pre, g_ple)):
                sp.dma_start(gate_in[:, i, :], g).then_inc(const_in, 16)
            for i, g in enumerate(gains):
                sp.dma_start(g_row[:, i, :], row_broadcast(g)).then_inc(const_in, 16)
            for t in range(1, TT):
                first_y(t)
            for C in range(NR4):
                sp.dma_start(w_raw[:, C, :], w_tail[NFF + C]).then_inc(w_dma[C], 16)
            for t in range(TT):
                sp.dma_start(res[:, t, :], x[t * P:(t + 1) * P, :]).then_inc(x_dma[t], 16)
            for C in range(NR4, NG1 + NR4):
                load_w(C, (NFF + C) if C < NG1 else C - NG1, C % NR4)

            def body(b, u, end=False):
                row = ((b + 1) % NBLK) * BT
                for i in range(NR4, NFF + NG3 if end else NCHB + NR4):
                    load_w(b * NCHB + (NG1 + i), i + NG1 if end and i >= NFF else i % NCHB, (u * NCHB + i) % NR4)
                    if i in LOAD_Y and not end:
                        load_y(b, row, LOAD_Y[i])
                    if i == P_AT - 8:
                        if end:
                            sp.wait_ge(p_lo, b + 1)
                        else:
                            sp.wait_ge(xn_done, turn_at(b) + 4)
                        sp.sem_inc(step, 1)
                        sp.dma_start(y_in[:].rearrange("p (c n) -> p c n", c=2),
                                     pT_d[:, bass.ds(b * BT, BT)].rearrange("(c p) n -> p c n", p=P)
                                     ).then_inc(y_dma, 16)
                    if end:
                        continue
                    t = i - (NFF + 7)
                    if 0 <= t < TT:
                        sp.wait_ge(h_done, h_at(b) + t + 1)
                        sp.dma_start(scr["h2"][t * P:(t + 1) * P, :], res[:, t, :]).then_inc(h2_out[t], 16)
                    if 1 <= t <= TT:
                        sp.wait_ge(xn_done, turn_at(b) + 4 + t)
                        sp.wait_ge(h2_out[t - 1], b * 16 + 16)
                        sp.sem_inc(step, 1)
                        sp.dma_start(res[:, t - 1, :], x[bass.ds(row + (t - 1) * P, P), :]).then_inc(x_dma[t - 1], 16)
                    if i in (NCHB - 3, NCHB - 2):
                        for t in (2 * (i - NCHB + 3), 2 * (i - NCHB + 3) + 1):
                            load_h2(b, t)
                for t in range(TT):
                    store_out(b, t)

            blocks(sp, body)
            for s in out_dma:
                sp.wait_ge(s, 16 * (NBLK + 2))
            for s in w_dma:
                sp.wait_ge(s, 16 * (NBLK * NCHB // NR4))

        @block.gpsimd
        def _(pool):
            pool.sem_inc(f_mul, 2)
            pool.sem_inc(o_done, 2)
            pool.sem_inc(p_lo, 1)

            def split(C, slot, half, nth):
                pool.wait_ge(w_dma[slot], nth * 16)
                if not (isinstance(C, int) and C < NSPL):
                    pool.wait_ge(w_used, C)
                pool.sem_inc(step, 1)
                pool.tensor_scalar(w_sp[0][:, half, :], w_raw[:, slot, :], 1.0, 0.0, ALU.mult, ALU.add).then_inc(w_hi, 1)
                pool.wait_ge(w_hi, C + 1)
                pool.tensor_tensor(w_sp[1][:, half, :], w_raw[:, slot, :], w_sp[0][:, half, :].bitcast(F32),
                                   ALU.subtract).then_inc(w_lo, 1)

            for C in range(NG1):
                split(C, C % NR4, C % NSPL, C // NR4 + 1)
            def two_blocks(it, count):
                for i in range(count):
                    split(it * (2 * NCHB) + (NG1 + i), i % NR4, i % NSPL,
                          it * (2 * NCHB // NR4) + (NG1 // NR4 + i // NR4 + 1))

            with pool.Fori(0, NBLK // 2 - 1) as it:
                two_blocks(it, 2 * NCHB)
            two_blocks(NBLK // 2 - 1, 2 * NCHB - NG1)

        @block.tensor
        def _(pe):
            def turn(i, t):
                pe.wait_ge(xn_done, i + 1)
                for half in range(2):
                    if not (isinstance(i, int) and i == 0):
                        pe.wait_ge(lo_done, i * 2 + half - 1)
                    for j in range(4):
                        kk = 4 * half + j
                        mm = pe.transpose(tp[half][:, j * P:(j + 1) * P], xn[:, t % 2, kk * P:(kk + 1) * P], ident[:])
                    mm.then_inc(tp_done, 1)

            def chunk(C, half, kind, b, what, xs, end=False):
                pe.wait_ge(w_lo, C + 1)
                first_of_chunk = [True]

                def product(dst, lhs, rhs, start, stop):
                    mm = pe.matmul(dst, lhs, rhs, start=start, stop=stop)
                    if first_of_chunk[0]:
                        mm.then_inc(w_used, 1)
                        first_of_chunk[0] = False
                    return mm

                if kind == "f":
                    g, j = what[0], what[1]
                    if g == 0 and j < 2:
                        pe.wait_ge(o_done, b * 8 + 2)
                    else:
                        pe.wait_ge(f_relu, f_at(b) + (NF * g + j - 1))
                    w = [a[:, half, :].rearrange("p (k n) -> p k n", k=KD) for a in w_sp]
                    for kk in range(KD):
                        for q, (a, m) in enumerate(PAIRS):
                            mm = product(fb[j % 2][:], w[a][:, kk, :], xs[m][:, kk, :],
                                         kk == 0 and q == 0, kk == KD - 1 and q == 2)
                    mm.then_inc(f_done, 1)
                    return
                g, n, pair = what
                w = [a[:, half, :].rearrange("p (k n) -> p k n", k=2) for a in w_sp]
                src = {"g2": fT, "ple": pT}.get(kind, xs)
                if kind == "g2" and n == 0:
                    pe.wait_ge(f_lo, f_at(b) + (NF * g + 2 * pair + 2))
                first, last = pair == 0, pair == 3 or kind == "ple"
                for t in range(TT):
                    dst = fb[t % 2][:] if kind == "ple" else acc[t][:]
                    if kind == "ple":
                        if not (n == 0 and t < 2):
                            pe.wait_ge(prod_done, b * 8 + (4 * n + t - 1))
                    elif first:
                        if kind == "g2" and g == 0:
                            pe.wait_ge(ev_act, act_at(b) + (4 * n - 4 + t + 1))
                        elif kind == "g2" and g == 1 and n == 0:
                            pe.wait_ge(ev_act, act_at(b) + (4 + t + 1))
                        elif kind == "g2":
                            pe.wait_ge(ev_dve, dve_at(b) + (8 * (g - 1) + 4 * n - 4 + t + 1))
                        elif kind == "g1" and n == 0:
                            if b is not None:
                                pe.wait_ge(ev_dve, dve_at(b) + (20 + t + 1))
                        elif kind == "g1":
                            pe.wait_ge(ev_act, t + 1 if b is None else act_at(b) + (8 + t + 1))
                        elif end and n == 0:
                            pe.wait_ge(ev_dve, dve_at(b) + (20 + t + 1))
                        else:
                            pe.wait_ge(ev_act, act_at(b) + ((4 if end else 12) + 4 * n + t + 1))
                    for kk in range(2):
                        for q, (a, m) in enumerate(PAIRS):
                            mm = product(dst, src[a][:, 2 * pair + kk, t * P:(t + 1) * P], w[m][:, kk, :],
                                         first and kk == 0 and q == 0, last and kk == 1 and q == 2)
                    if last:
                        mm.then_inc(ple_done if kind == "ple" else acc_done, 1)

            pe.wait_ge(const_in, 96)
            for t in range(TT):
                turn(t, t)
            pe.wait_ge(lo_done, 2 * TT)
            for C, c in enumerate(G1):
                chunk(C, C % NSPL, c[0], None, c[1:], xT[1])
            for t in range(TT):
                turn(TT + t, t)

            def body(b, u, end=False):
                C = b * NCHB + NG1
                pe.wait_ge(lo_done, turn_at(b) * 2)
                for i, c in enumerate(FF):
                    chunk(C + i, i % NSPL, c[0], b, c[1:], xT[u])
                    if i in TURN_Y and not end:
                        turn(turn_at(b) + TURN_Y[i], TURN_Y[i])
                if end:
                    for t in range(TT):
                        turn(turn_at(b) + t, t)
                    pe.wait_ge(lo_done, turn_at(b) * 2 + 8)
                    pe.wait_ge(p_lo, b + 2)
                    for i, c in enumerate(G3):
                        chunk(C + (NFF + i), (NFF + i) % NSPL, c[0], b, c[1:], xT[u], True)
                    return
                pe.wait_ge(lo_done, turn_at(b) * 2 + 8)
                for i, c in enumerate(G1):
                    chunk(C + (NFF + i), (NFF + i) % NSPL, c[0], b, c[1:], xT[1 - u])
                    if i in TURN_Z:
                        turn(turn_at(b) + (4 + TURN_Z[i]), TURN_Z[i])
                pe.wait_ge(lo_done, turn_at(b) * 2 + 16)
                pe.wait_ge(p_lo, b + 2)
                for i, c in enumerate(G3):
                    at = NFF + NG1 + i
                    chunk(C + at, at % NSPL, c[0], b, c[1:], xT[u])
                    if i in TURN_X:
                        turn(turn_at(b) + (8 + TURN_X[i]), TURN_X[i])

            blocks(pe, body)

        @block.scalar
        def _(act):
            def root(i, slot, parts):
                act.wait_ge(rec_done, i + 1)
                act.activation(rstd[:, slot, 0:parts], rec[:, slot, 0:parts], ACT.Sqrt).then_inc(rt_done, 1)

            def norms(at, h0, sums_read):
                def square(n):
                    place, t = SQUARES[n]
                    if place == 1:
                        act.wait_ge(*sums_read(t))
                    else:
                        act.wait_ge(h_done, h0 + (t + 1))
                    act.activation(junk[:, n % 2, :], (total if place == 1 else res)[:, t, :], ACT.Square,
                                   accum_out=ssq[:, TT + n, 0:1]).then_inc(sq_done, 1)

                for what, n in (("s", 0), ("s", 1), ("r", 0), ("r", 1), ("s", 2), ("s", 3), ("r", 2), ("s", 4), ("r", 3),
                                ("s", 5), ("r", 4), ("r", 5), ("s", 6), ("s", 7), ("r", 6), ("r", 7)):
                    if what == "s":
                        square(n)
                    else:
                        root(at + n, TT + n, 1)

            def y_norm(i, t, loaded, src):
                act.wait_ge(*loaded)
                for part in range(2):
                    at = slice(part * D_AB, (part + 1) * D_AB)
                    ins = act.activation(junk[:, 0, at], src[:, at], ACT.Square, accum_out=ssq[:, t % 4, part:part + 1])
                ins.then_inc(sq_done, 1)
                root(i, t % 4, 2)

            def turned_hi(i, t, gain, dst):
                for half in range(2):
                    act.wait_ge(tp_done, i * 2 + half + 1)
                    for j in range(4):
                        kk = 4 * half + j
                        ins = act.activation(dst[0][:, kk, t * P:(t + 1) * P], tp[half][:, j * P:(j + 1) * P], ACT.Copy,
                                             scale=gate_in[:, gain, kk:kk + 1])
                    ins.then_inc(hi_done, 1)

            def to_total(count, n, t):
                act.wait_ge(acc_done, count)
                act.activation(total[:, t, n * BANK:(n + 1) * BANK], acc[t][:], ACT.Copy).then_inc(ev_act, 1)

            for t in range(TT + 1):
                if t < TT:
                    y_norm(t, t, (out_dma[t], 32), total[:, t, :])
                if t == 0:
                    act.wait_ge(const_in, 96)
                else:
                    turned_hi(t - 1, t - 1, 0, xT[1])
            for n in range(2):
                for t in range(TT):
                    to_total(4 * n + t + 1, n, t)
            norms(4, 0, lambda t: (ev_act, 4 + t + 1))
            for t in range(TT):
                turned_hi(TT + t, t, 1, xT[0])

            def body(b, u, end=False):
                def hidden(g, j):
                    F = f_at(b) + (NF * g + j)
                    act.wait_ge(f_done, F + 1)
                    if g == 0 and j < 2:
                        act.wait_ge(o_done, b * 8 + 2)
                    act.wait_ge(f_mul, F + 1)
                    act.activation(rl[:, j % 2, :], fb[j % 2][:], ACT.Relu).then_inc(f_relu, 1)
                    act.wait_ge(f_relu, F + 1)
                    act.activation(fT[0][:, j, :], rl[:, j % 2, :], ACT.Square).then_inc(f_hi, 1)

                for i, c in enumerate(FF):
                    if c[0] == "f":
                        hidden(c[1], c[2])
                    elif c[1] == 0 and c[3] == 3:
                        for t in range(TT):
                            if c[2] == 0:
                                act.wait_ge(out_dma[t], b * 16 + 32)
                            to_total(acc_at(b) + (4 * c[2] + t + 1), c[2], t)
                    if i in NORM_Y and not end:
                        t = NORM_Y[i]
                        y_norm(norm_at(b) + t, t, (y_dma, b * 144 + 32 * (t + 1)), y_in)
                    if i in TURN_Y and not end:
                        t = TURN_Y[i]
                        turned_hi(turn_at(b) + t, t, 0, xT[1 - u])
                    if i == P_AT:
                        act.wait_ge(y_dma, b * 144 + (16 if end else 32 * TT + 16))
                        act.activation(pT[0][:].rearrange("p c n -> p (c n)"), y_in[:], ACT.Copy).then_inc(p_hi, 1)

                def gates(n):
                    for t in range(TT):
                        q = 4 * n + t
                        act.wait_ge(acc_done, acc_at(b) + ((32 if end else 40) + q + 1))
                        if q < 2:
                            act.wait_ge(f_mul, f_at(b) + (4 * NF + 2))
                        else:
                            act.wait_ge(prod_done, b * 8 + (q - 1))
                        act.activation(rl[:, t % 2, :], acc[t][:], ACT.Sigmoid).then_inc(ev_act, 1)

                z_hi = lambda t: turned_hi(turn_at(b) + ((0 if end else 4) + t), t, 2, xT[u])
                x_hi = lambda t: turned_hi(turn_at(b) + (8 + t), t, 1, xT[1 - u])
                norms(norm_at(b) + (0 if end else 4), h_at(b), lambda t: (ev_dve, dve_at(b) + (20 + t + 1)))
                if end:
                    for t in range(TT):
                        z_hi(t)
                    gates(0)
                    gates(1)
                    return
                z_hi(0)
                for t in range(TT):
                    to_total(acc_at(b) + (32 + t + 1), 0, t)
                z_hi(1)
                z_hi(2)
                z_hi(3)
                for t in range(TT):
                    to_total(acc_at(b) + (36 + t + 1), 1, t)

                norms(norm_at(b) + 12, h_at(b) + 4, lambda t: (ev_act, act_at(b) + (12 + t + 1)))
                x_hi(0)
                x_hi(1)
                gates(0)
                x_hi(2)
                x_hi(3)
                gates(1)

            blocks(act, body)

        @block.vector
        def _(ve):
            def inverse(i, slot, parts, width):
                ve.wait_ge(sq_done, i + 1)
                ve.tensor_scalar(ms[:, slot, 0:parts], ssq[:, slot, 0:parts], 1.0 / width, EPS, ALU.mult, ALU.add
                                 ).then_inc(var_done, 1)
                ve.wait_ge(var_done, i + 1)
                ve.reciprocal(rec[:, slot, 0:parts], ms[:, slot, 0:parts]).then_inc(rec_done, 1)

            def normed(i, slot, T, t, src, parts=1):
                ve.wait_ge(rt_done, i + 1)
                if not (isinstance(T, int) and T < 2):
                    ve.wait_ge(tp_done, T * 2 - 2)
                for part in range(parts):
                    at = slice(part * (D // parts), (part + 1) * (D // parts))
                    ins = ve.tensor_scalar(xn[:, t % 2, at], src[:, at], rstd[:, slot, part:part + 1], None, ALU.mult)
                ins.then_inc(xn_done, 1)

            def turned_lo(i, t, gain, dst):
                for half in range(2):
                    ve.wait_ge(hi_done, i * 2 + half + 1)
                    for j in range(4):
                        kk = 4 * half + j
                        at = (slice(None), kk, slice(t * P, (t + 1) * P))
                        ins = ve.scalar_tensor_tensor(out=dst[1][at], in0=tp[half][:, j * P:(j + 1) * P],
                                                      scalar=gate_in[:, gain, kk:kk + 1], in1=dst[0][at].bitcast(F32),
                                                      op0=ALU.mult, op1=ALU.subtract)
                    ins.then_inc(lo_done, 1)

            def residuals(at, h0, which, T, x_read, lo):
                def inv(n):
                    inverse(at + n, TT + n, 1, D)

                def added(t):
                    n = SQUARES.index((1, t))
                    ve.wait_ge(rt_done, at + n + 1)
                    if x_read is not None:
                        ve.wait_ge(x_dma[t], x_read)
                    ve.scalar_tensor_tensor(out=total[:, t, :], in0=total[:, t, :], scalar=rstd[:, TT + n, 0:1],
                                            in1=g_row[:, which, :], op0=ALU.mult, op1=ALU.mult).then_inc(gained, 1)
                    ve.wait_ge(gained, h0 + (t + 1))
                    ve.tensor_tensor(res[:, t, :], res[:, t, :], total[:, t, :], ALU.add).then_inc(h_done, 1)

                def unit(t):
                    n = SQUARES.index((2, t))
                    normed(at + n, TT + n, T + t, t, res[:, t, :])

                for what, n in ((inv, 0), (inv, 1), (added, 0), (inv, 2), (added, 1), (inv, 3), (added, 2), (inv, 4),
                                (inv, 5), (added, 3), (unit, 0), (unit, 1), (inv, 6), (inv, 7), (lo, 0), (unit, 2),
                                (lo, 1), (unit, 3)):
                    what(n)

            for t in range(TT + 1):
                if t < TT:
                    inverse(t, t, 2, D_AB)
                    normed(t, t, t, t, total[:, t, :], 2)
                if t == 0:
                    ve.wait_ge(const_in, 96)
                else:
                    turned_lo(t - 1, t - 1, 0, xT[1])
            first_lo = lambda t: turned_lo(TT + t, t, 1, xT[0])
            residuals(4, 0, 0, TT, 16, first_lo)
            first_lo(2)
            first_lo(3)

            def body(b, u, end=False):
                def hidden(g, j):
                    F = f_at(b) + (NF * g + j)
                    ve.wait_ge(f_relu, F + 1)
                    ve.tensor_tensor(fs[:, j % 2, :], rl[:, j % 2, :], rl[:, j % 2, :], ALU.mult).then_inc(f_mul, 1)
                    ve.wait_ge(f_mul, F + 3)
                    ve.wait_ge(f_hi, F + 1)
                    ve.tensor_tensor(fT[1][:, j, :], fs[:, j % 2, :], fT[0][:, j, :].bitcast(F32), ALU.subtract
                                     ).then_inc(f_lo, 1)

                for i, c in enumerate(FF):
                    if c[0] == "f":
                        hidden(c[1], c[2])
                    elif c[1] > 0 and c[3] == 3:
                        for t in range(TT):
                            q = 4 * c[2] + t
                            ve.wait_ge(acc_done, acc_at(b) + (8 * c[1] + q + 1))
                            if c[1] == 1:
                                ve.wait_ge(ev_act, act_at(b) + (q + 1))
                            else:
                                ve.wait_ge(ev_dve, dve_at(b) + (8 * (c[1] - 2) + q + 1))
                            at = total[:, t, c[2] * BANK:(c[2] + 1) * BANK]
                            ve.tensor_tensor(at, acc[t][:], at, ALU.add).then_inc(ev_dve, 1)
                    if i in NORM_Y and not end:
                        t = NORM_Y[i]
                        inverse(norm_at(b) + t, t, 2, D_AB)
                        normed(norm_at(b) + t, t, turn_at(b) + t, t, y_in[:], 2)
                    if i in TURN_Y and not end:
                        t = TURN_Y[i]
                        turned_lo(turn_at(b) + t, t, 0, xT[1 - u])
                    if i == P_AT:
                        ve.wait_ge(p_hi, b + 1)
                        ve.tensor_tensor(pT[1][:].rearrange("p c n -> p (c n)"), y_in[:],
                                         pT[0][:].rearrange("p c n -> p (c n)").bitcast(F32), ALU.subtract
                                         ).then_inc(p_lo, 1)

                z_at = turn_at(b) + (0 if end else 4)
                z_lo = lambda t: turned_lo(z_at + t, t, 2, xT[u])
                x_lo = lambda t: turned_lo(turn_at(b) + (8 + t), t, 1, xT[1 - u])
                residuals(norm_at(b) + (0 if end else 4), h_at(b), 1, z_at, None, z_lo)
                z_lo(2)
                z_lo(3)

                def outputs(n):
                    for t in range(TT):
                        q = 4 * n + t
                        ve.wait_ge(ev_act, act_at(b) + ((8 if end else 16) + q + 1))
                        ve.wait_ge(ple_done, b * 8 + (q + 1))
                        ve.tensor_tensor(fs[:, t % 2, :], fb[t % 2][:], rl[:, t % 2, :], ALU.mult).then_inc(prod_done, 1)
                        ve.wait_ge(prod_done, b * 8 + (q + 1))
                        if n == 0 and not end:
                            ve.wait_ge(h2_in[t], b * 16 + 16)
                        at = (slice(None), t, slice(n * BANK, (n + 1) * BANK))
                        ve.tensor_tensor(total[at], fs[:, t % 2, :], (res if end else total)[at], ALU.add
                                         ).then_inc(o_done, 1)

                if end:
                    outputs(0)
                    outputs(1)
                    return
                residuals(norm_at(b) + 12, h_at(b) + 4, 0, turn_at(b) + 8, b * 16 + 32, x_lo)
                outputs(0)
                x_lo(2)
                x_lo(3)
                outputs(1)

            blocks(ve, body)


def chunked(w, half_k, width):
    kk, n = w.shape[0] // P, w.shape[1] // width
    a = w.reshape(kk // half_k, half_k, P, n, width).transpose(3, 0, 2, 1, 4)
    return a.reshape(-1, P, half_k * width)


def token_order():
    return np.arange(S).reshape(SUB, RES).T.reshape(-1)


def rope_constants():
    grid = 64
    tok = token_order()
    n_axis = HD // 4
    inv = np.float32(10000.0) ** (-np.arange(n_axis, dtype=np.float32) / np.float32(n_axis))
    row, col = (tok // grid).astype(np.float32), (tok % grid).astype(np.float32)
    ang = np.concatenate([row[:, None] * inv, col[:, None] * inv], -1).astype(np.float32)
    cos, sin = np.cos(ang), np.sin(ang)
    return np.concatenate([cos, cos, -sin, sin], -1).astype(np.float32)


def bias_constants():
    m = np.arange(2 * BANK) - (BANK - 1)
    onehot = np.zeros((32, 8, 2 * BANK), np.float32)
    log_count = np.full((8, 2 * BANK), NEG, np.float32)
    for v, diff in enumerate((-3, -2, -1, None, 1, 2, 3, 0)):
        if diff is None:
            continue
        rel = RES * m + diff
        dist = np.abs(rel)
        count = (dist <= 64) * 1 + ((dist <= 256) & (rel % 4 == 0)) + ((dist <= 1024) & (rel % 16 == 0))
        large = 8 + (np.log(np.maximum(dist, 8).astype(np.float32) / np.float32(8)) / np.float32(math.log(128.0))
                     * np.float32(8)).astype(np.int32)
        bucket = np.where(rel > 0, 16, 0) + np.where(dist < 8, dist, np.minimum(large, 15))
        held = count > 0
        log_count[v, held] = np.log(count[held].astype(np.float64))
        onehot[bucket[held], v, np.flatnonzero(held)] = 1.0
    both = np.concatenate([onehot, log_count[None]], 0)
    near = both[:, 0:7, BANK - PAD - P:BANK + PAD + P]
    return np.concatenate([both[:, 7], near.reshape(33, -1)], 1)


def lay_out(x, p, w_in, g_attn_pre, g_q, g_k, g_out_a, g_out_b, w_out, g_attn_post, rel_bias,
            g_mlp_pre, w_ff1, w_ff2, g_mlp_post, g_ple, w_ple_gate, w_ple_proj):
    order = token_order()
    xo = x[0][order]
    w = w_in[0]
    by_tile = lambda g: g.reshape(KD, P).T
    ff = [a for g in range(0, D_FF, D) for a in (chunked(w_ff1[0][:, g:g + D], KD, P),
                                                  chunked(w_ff2[0][g:g + D], 2, BANK))]
    gate, ple = chunked(w_ple_gate[0], 2, BANK), chunked(w_ple_proj[0], 2, BANK)
    return {
        "rel_bias": np.concatenate([rel_bias, np.ones((1, NHB), np.float32)], 0),
        "onehot": bias_constants(),
        "x": np.concatenate([xo, xo[:BT]], 0),
        "w_in": np.concatenate([chunked(w[:, 0:512], 4, 512), chunked(w[:, 512:768], 8, 256),
                                chunked(w[:, 768:], 4, 512)], 0),
        "rope": rope_constants(),
        "ident": np.eye(P, dtype=np.float32),
        "fold": np.concatenate([np.eye(HD, dtype=np.float32)] * 2, 0),
        "w_tail": np.concatenate(ff + [chunked(w_out[0], 2, BANK), gate[:4], ple[:1], gate[4:], ple[1:]], 0),
        "g_out": by_tile(np.concatenate([g_out_a[0], g_out_b[0]])),
        "g_mlp_pre": by_tile(g_mlp_pre[0]),
        "g_ple": by_tile(g_ple[0]),
        "g_attn_pre": g_attn_pre[0], "g_q": g_q[0], "g_k": g_k[0],
        "g_attn_post": g_attn_post[0], "g_mlp_post": g_mlp_post[0],
        "pT": p[0, 0][order].T,
    }


def layer(nc, rel_bias, onehot, x, w_in, rope, ident, fold, w_tail, g_out, g_mlp_pre, g_ple,
          g_attn_pre, g_q, g_k, g_attn_post, g_mlp_post, pT, out):
    shapes = {"qA": (S, NHA * 2 * HD), "kA": (S, NKV * 2 * HD), "vA": (S, NKV * HD), "qB": (S, 2 * D_AB), "kB": (S, 2 * D_AB),
              "vB": (S + 2 * PAD, D_AB), "bias": (NHB, ROWS_W), "table": (NHB, P, ROWS_W),
              "yA": (S + P, D_AB), "yB": (S, D_AB), "h2": (BT, D)}
    scr = {n: nc.dram_tensor(f"scr_{n}", shape, F32, kind="Internal").ap() for n, shape in shapes.items()}
    with nc.semaphore("step") as step:
        project_phase(nc, x, w_in, g_attn_pre, g_q, g_k, rope, ident, rel_bias, onehot, scr, step)
        mixer_a_phase(nc, ident, fold, scr)
        mixer_b_phase(nc, ident, fold, scr, step)
        feed_phase(nc, x, w_tail, (g_attn_post, g_mlp_post), g_out, g_mlp_pre, g_ple, pT, ident, scr, out, step)


def kernel(**inputs):
    import numpy as _np
    import concourse.bacc as _bacc
    from concourse import mybir as _mybir
    from concourse.bass_utils import run_bass_kernel_spmd as _run

    nc = _bacc.Bacc("TRN2", target_bir_lowering=False, num_devices=1)
    arrays = {f"{n}_dram": _np.ascontiguousarray(a) for n, a in
              lay_out(**{n: _np.asarray(a) for n, a in inputs.items()}).items()}
    args = [nc.dram_tensor(n, a.shape, _mybir.dt.from_np(a.dtype), kind="ExternalInput").ap() for n, a in arrays.items()]
    out = nc.dram_tensor("out_dram", (S, D), _mybir.dt.float32, kind="ExternalOutput").ap()
    layer(nc, *args, out)
    got = _run(nc, [arrays], core_ids=[0]).results[0]["out_dram"]
    y = _np.empty_like(got)
    y[token_order()] = got
    return y[None]
```
